# Optimizing a Trainium2 kernel written in Bass

```python
import math
import jax, jax.numpy as jnp
from jax import lax
import numpy as np

D_MODEL = 2048
BATCH = 1
SEQ = 512
DEPTH = 1
DEC_BATCH = 8
DEC_SEQ = 4
PAST_LEN = 2048
PAGE_SIZE = 128

MIX_WIDTH = D_MODEL
GLA_HEADS = 4
GLA_DV = (MIX_WIDTH // 2) // GLA_HEADS
GLA_DK = GLA_DV // 2
GLA_GATE_RANK = 16
GLA_TAU = 16.0
GLA_CHUNK = 64
GLA_QK_W = GLA_HEADS * GLA_DK
GLA_V_W = GLA_HEADS * GLA_DV
SWA_HEADS = 8
SWA_HD = (MIX_WIDTH // 2) // SWA_HEADS
SWA_W = SWA_HEADS * SWA_HD
SWA_PATTERNS = ((128, 1), (512, 4), (2048, 16))
SWA_MAX_WINDOW = 2048
D_FF = 5632
CONV_W = 3
EPS = 1e-6

IN_SIZES = (GLA_QK_W, GLA_QK_W, GLA_V_W, GLA_V_W, GLA_GATE_RANK, SWA_W, SWA_W, SWA_W)
IN_COLS = sum(IN_SIZES)

kernel_name = "hybrid_gla_dilated_swa_convffn_step"

F32 = jnp.float32

def rms_norm(x, g):
    xf = x.astype(F32)
    y = xf * lax.rsqrt(jnp.mean(xf * xf, axis=-1, keepdims=True) + EPS) * g.astype(F32)
    return y.astype(x.dtype)

def alibi_slopes(n):
    return 2.0 ** (-8.0 * jnp.arange(1, n + 1, dtype=F32) / n)

def gla_recurrence(q, k, v, log_a, s0):
    b, t, h, dk = q.shape
    dv = v.shape[-1]
    c = min(GLA_CHUNK, t)
    n = -(-t // c)
    pad = n * c - t
    q, k, v, log_a = [a.astype(F32) for a in (q, k, v, log_a)]
    if pad:
        padw = ((0, 0), (0, pad), (0, 0), (0, 0))
        q, k, v, log_a = [jnp.pad(a, padw) for a in (q, k, v, log_a)]

    def blocks(a):
        return a.reshape(b, n, c, h, a.shape[-1]).transpose(1, 0, 3, 2, 4)

    qc, kc, vc, gc = map(blocks, (q, k, v, log_a))
    cum = jnp.cumsum(gc, axis=3)
    total = cum[:, :, :, -1:, :]
    q_dec = qc * jnp.exp(cum)
    k_dec = kc * jnp.exp(-cum)
    k_to_end = kc * jnp.exp(total - cum)
    causal = jnp.tril(jnp.ones((c, c), dtype=bool))
    attn = jnp.where(causal, jnp.einsum('nbhtd,nbhsd->nbhts', q_dec, k_dec), 0.0)
    o_intra = jnp.einsum('nbhts,nbhsv->nbhtv', attn, vc)

    def step(s, inp):
        qd, kte, vv, tot = inp
        o_inter = jnp.einsum('bhtd,bhdv->bhtv', qd, s)
        s_new = s * jnp.exp(tot[:, :, 0, :])[..., None] + jnp.einsum('bhsd,bhsv->bhdv', kte, vv)
        return s_new, o_inter

    s_fin, o_inter = lax.scan(step, s0.astype(F32), (q_dec, k_to_end, vc, total))
    o = (o_intra + o_inter).transpose(1, 0, 3, 2, 4).reshape(b, n * c, h, dv)[:, :t]
    return o, s_fin

def dilated_branch_prompt(q, k, v, window, dil, slopes):
    b, t, h, hd = q.shape
    n = window // dil
    L = t // dil
    nb = -(-L // n)
    pad = nb * n - L

    def by_residue(a):
        a = a.reshape(b, L, dil, h, hd).transpose(0, 2, 3, 1, 4)
        a = jnp.pad(a, ((0, 0), (0, 0), (0, 0), (0, pad), (0, 0)))
        return a.reshape(b, dil, h, nb, n, hd)

    def with_prev(a):
        prev = jnp.pad(a, ((0, 0), (0, 0), (0, 0), (1, 0), (0, 0), (0, 0)))[:, :, :, :-1]
        return jnp.concatenate([prev, a], axis=4)

    qb = by_residue(q)
    k2 = with_prev(by_residue(k))
    v2 = with_prev(by_residue(v))
    s = jnp.einsum('brhnqd,brhnkd->brhnqk', qb, k2) * (SWA_HD ** -0.5)
    steps = jnp.arange(n)[:, None] + n - jnp.arange(2 * n)[None, :]
    blk = jnp.arange(nb)[:, None, None]
    valid = (steps >= 0) & (steps <= n) & (blk * n + jnp.arange(2 * n)[None, None, :] - n >= 0)
    s = s - slopes[:, None, None, None] * (dil * steps).astype(F32)
    s = jnp.where(valid, s, -jnp.inf)
    lse = jax.nn.logsumexp(s, axis=-1)
    o = jnp.einsum('brhnqk,brhnkd->brhnqd', jnp.exp(s - lse[..., None]), v2)

    def back(a):
        a = a.reshape((b, dil, h, nb * n) + a.shape[5:])[:, :, :, :L]
        a = jnp.moveaxis(a, 3, 1)
        return a.reshape((b, t, h) + a.shape[4:])

    return back(o), back(lse)

def dilated_branch_sample(q, k_all, v_all, window, dil, slopes):
    b, tn, h, hd = q.shape
    w_rows = k_all.shape[1] - tn
    n = window // dil
    steps = jnp.arange(n + 1)
    idx = w_rows + jnp.arange(tn)[:, None] - dil * steps[None, :]
    valid = idx >= 0
    idx = jnp.clip(idx, 0)
    kg = k_all[:, idx]
    vg = v_all[:, idx]
    s = jnp.einsum('bqhd,bqkhd->bhqk', q, kg) * (SWA_HD ** -0.5)
    s = s - slopes[:, None, None] * (dil * steps).astype(F32)
    s = jnp.where(valid, s, -jnp.inf)
    lse = jax.nn.logsumexp(s, axis=-1)
    o = jnp.einsum('bhqk,bqkhd->bqhd', jnp.exp(s - lse[..., None]), vg)
    return o, lse.transpose(0, 2, 1)

def combine_branches(outs, lses):
    w = jax.nn.softmax(jnp.stack(lses), axis=0)
    return jnp.einsum('gbth,gbthd->bthd', w, jnp.stack(outs))

def conv_ffn(x, conv_s0, w_up, w_conv, b_conv, w_down):
    t = x.shape[1]
    u = x @ w_up
    u_ext = jnp.concatenate([conv_s0.astype(u.dtype), u], axis=1)
    c = b_conv
    for j in range(CONV_W):
        c = c + w_conv[j] * u_ext[:, j:j + t]
    a, val = jnp.split(c, 2, axis=-1)
    y = (jax.nn.silu(a) * val) @ w_down
    return y, u_ext[:, t:]

def hybrid_layer(x, gla_s0, conv_s0, swa_past, g_attn_norm, w_in, w_gate_up, b_gate, g_gla_norm, w_out,
                 g_ffn_norm, w_up, w_conv, b_conv, w_down):
    b, t, _ = x.shape
    xn = rms_norm(x, g_attn_norm)
    proj = xn @ w_in
    qa, ka, va, ga, za, qb, kb, vb = jnp.split(proj, list(np.cumsum(IN_SIZES)[:-1]), axis=-1)

    log_a = jax.nn.log_sigmoid((za @ w_gate_up + b_gate).astype(F32)) / GLA_TAU
    o_a, s_a = gla_recurrence(
        qa.reshape(b, t, GLA_HEADS, GLA_DK).astype(F32) * (GLA_DK ** -0.5),
        ka.reshape(b, t, GLA_HEADS, GLA_DK),
        va.reshape(b, t, GLA_HEADS, GLA_DV),
        log_a.reshape(b, t, GLA_HEADS, GLA_DK),
        gla_s0)
    o_a = rms_norm(o_a, g_gla_norm.reshape(GLA_HEADS, GLA_DV)).reshape(b, t, GLA_V_W)
    o_a = (o_a * jax.nn.silu(ga.astype(F32))).astype(x.dtype)

    qh = qb.reshape(b, t, SWA_HEADS, SWA_HD)
    kh = kb.reshape(b, t, SWA_HEADS, SWA_HD)
    vh = vb.reshape(b, t, SWA_HEADS, SWA_HD)
    slopes = alibi_slopes(SWA_HEADS)
    if swa_past is None:
        qf, kf, vf = qh.astype(F32), kh.astype(F32), vh.astype(F32)
        res = [dilated_branch_prompt(qf, kf, vf, w, d, slopes) for (w, d) in SWA_PATTERNS]
        keep = min(SWA_MAX_WINDOW, t)
        k_buf, v_buf = kh[:, t - keep:], vh[:, t - keep:]
    else:
        k_all = jnp.concatenate([swa_past[0].astype(kh.dtype), kh], axis=1)
        v_all = jnp.concatenate([swa_past[1].astype(vh.dtype), vh], axis=1)
        qf, kf, vf = qh.astype(F32), k_all.astype(F32), v_all.astype(F32)
        res = [dilated_branch_sample(qf, kf, vf, w, d, slopes) for (w, d) in SWA_PATTERNS]
        keep = min(SWA_MAX_WINDOW, k_all.shape[1])
        k_buf, v_buf = k_all[:, k_all.shape[1] - keep:], v_all[:, v_all.shape[1] - keep:]
    o_b = combine_branches([r[0] for r in res], [r[1] for r in res]).reshape(b, t, SWA_W).astype(x.dtype)

    h = x + jnp.concatenate([o_a, o_b], axis=-1) @ w_out
    f, conv_new = conv_ffn(rms_norm(h, g_ffn_norm), conv_s0, w_up, w_conv, b_conv, w_down)
    return h + f, s_a, k_buf, v_buf, conv_new

def setup_inputs(seed: int = 0) -> dict:
    key = jax.random.key(seed)
    ks = jax.random.split(key, 20)
    w_past = min(SWA_MAX_WINDOW, PAST_LEN)
    nrm = lambda k, shape: jax.random.normal(k, shape, F32)
    return {
        "x_prompt": nrm(ks[0], (BATCH, SEQ, D_MODEL)),
        "x_sample": nrm(ks[1], (DEC_BATCH, DEC_SEQ, D_MODEL)),
        "state_gla": nrm(ks[2], (DEPTH, DEC_BATCH, GLA_HEADS, GLA_DK, GLA_DV)),
        "cache_swa_k": nrm(ks[3], (DEPTH, DEC_BATCH, w_past, SWA_HEADS, SWA_HD)),
        "cache_swa_v": nrm(ks[4], (DEPTH, DEC_BATCH, w_past, SWA_HEADS, SWA_HD)),
        "state_ffn_conv": nrm(ks[5], (DEPTH, DEC_BATCH, CONV_W - 1, 2 * D_FF)),
        "g_attn_norm": 1.0 + 0.02 * nrm(ks[6], (DEPTH, D_MODEL)),
        "w_in": nrm(ks[7], (DEPTH, D_MODEL, IN_COLS)) * D_MODEL ** -0.5,
        "w_gate_up": nrm(ks[8], (DEPTH, GLA_GATE_RANK, GLA_QK_W)) * GLA_GATE_RANK ** -0.5,
        "b_gate": 0.1 * nrm(ks[9], (DEPTH, GLA_QK_W)),
        "g_gla_norm": 1.0 + 0.02 * nrm(ks[10], (DEPTH, GLA_V_W)),
        "w_out": nrm(ks[11], (DEPTH, MIX_WIDTH, D_MODEL)) * MIX_WIDTH ** -0.5,
        "g_ffn_norm": 1.0 + 0.02 * nrm(ks[12], (DEPTH, D_MODEL)),
        "w_up": nrm(ks[13], (DEPTH, D_MODEL, 2 * D_FF)) * D_MODEL ** -0.5,
        "w_conv": nrm(ks[14], (DEPTH, CONV_W, 2 * D_FF)) * CONV_W ** -0.5,
        "b_conv": 0.02 * nrm(ks[15], (DEPTH, 2 * D_FF)),
        "w_down": nrm(ks[16], (DEPTH, D_FF, D_MODEL)) * D_FF ** -0.5,
        "g_final": 1.0 + 0.02 * nrm(ks[17], (D_MODEL,)),
    }

def reference(x_prompt, x_sample, state_gla, cache_swa_k, cache_swa_v, state_ffn_conv,
              g_attn_norm, w_in, w_gate_up, b_gate, g_gla_norm, w_out,
              g_ffn_norm, w_up, w_conv, b_conv, w_down, g_final):
    yp, ys = x_prompt, x_sample
    gla_p, gla_s, kp, ksm, vp, vsm, cp, csm = [], [], [], [], [], [], [], []
    for l in range(DEPTH):
        params = (g_attn_norm[l], w_in[l], w_gate_up[l], b_gate[l], g_gla_norm[l], w_out[l],
                  g_ffn_norm[l], w_up[l], w_conv[l], b_conv[l], w_down[l])
        gla0 = jnp.zeros((yp.shape[0], GLA_HEADS, GLA_DK, GLA_DV), F32)
        conv0 = jnp.zeros((yp.shape[0], CONV_W - 1, 2 * D_FF), yp.dtype)
        yp, s1, k1, v1, c1 = hybrid_layer(yp, gla0, conv0, None, *params)
        ys, s2, k2, v2, c2 = hybrid_layer(ys, state_gla[l], state_ffn_conv[l],
                                          (cache_swa_k[l], cache_swa_v[l]), *params)
        gla_p.append(s1); gla_s.append(s2)
        kp.append(k1); ksm.append(k2)
        vp.append(v1); vsm.append(v2)
        cp.append(c1); csm.append(c2)
    y_prompt = rms_norm(yp, g_final)
    y_sample = rms_norm(ys, g_final)
    state_gla_prompt = jnp.stack(gla_p)
    state_gla_sample = jnp.stack(gla_s)
    cache_swa_k_prompt = jnp.stack(kp)
    cache_swa_k_sample = jnp.stack(ksm)
    cache_swa_v_prompt = jnp.stack(vp)
    cache_swa_v_sample = jnp.stack(vsm)
    state_ffn_conv_prompt = jnp.stack(cp)
    state_ffn_conv_sample = jnp.stack(csm)
    return (y_prompt, y_sample, state_gla_prompt, state_gla_sample, cache_swa_k_prompt, cache_swa_k_sample,
            cache_swa_v_prompt, cache_swa_v_sample, state_ffn_conv_prompt, state_ffn_conv_sample)


_drawn_inputs = setup_inputs


def setup_inputs(seed=0):
    import zlib

    import numpy as np

    out = dict(_drawn_inputs(seed))
    spreads = {}
    factors = {'g_gla_norm': 6.993, 'g_ffn_norm': 2.938, 'b_conv': 4.219, 'g_final': 2.822}
    for name, (base, spread) in spreads.items():
        noise = np.random.default_rng([zlib.crc32(name.encode()), seed]).standard_normal(out[name].shape)
        drawn = base * np.exp(spread * noise) if base else spread * noise
        out[name] = __import__('jax').numpy.asarray(drawn.astype(out[name].dtype))
    for name, factor in factors.items():
        out[name] = (out[name] * factor).astype(out[name].dtype)
    return out
```

```python
import math

import concourse.bass as bass
import numpy as np
from concourse import mybir

F32 = mybir.dt.float32
F32R = mybir.dt.float32r
ACT = mybir.ActivationFunctionType
ALU = mybir.AluOpType

P = 128
D = 2048
KT = D // P
SEQ, NB, NQ = 512, 8, 4
SAMP = NB * NQ
T = SEQ + SAMP
HALF = T // 2
HEADS, HD = 8, 128
GH, DK, DV = 4, 128, 256
CH = 64
NCH = SEQ // CH
RANK = 16
TAU = 16.0
DFF = 5632
FT = DFF // P
GT = 4
NG = FT // GT
PAST = 2048
EPS = 1e-6
SCALE = float(HD) ** -0.5
UNIT = 2048

C_QA, C_KA, C_VA, C_GA, C_ZA = 0, 512, 1024, 2048, 3072
C_QB = C_ZA + RANK
C_KB, C_VB = C_QB + 1024, C_QB + 2048
IN_COLS = C_VB + 1024

U_GLA = 3 * HEADS
U_OUT = U_GLA + 6 * GH
U_FFN = U_OUT + KT
PAIR = 2 * GT
DOWN = 4

NEAR = 512
FAR = (PAST - NEAR) // 16
NKEY = NEAR + 4 * FAR + SAMP
NEG = -1.0e30

CHUNK_ROWS = 146
COPIES = (PAST - NQ) // CHUNK_ROWS


def at(c, it=None, k=0):
    return c if it is None else it * k + c


class Order:

    def __init__(self, eng, sem):
        self.eng, self.sem, self.base, self.n = eng, sem, 0, 0

    def mark(self, ins):
        ins.then_inc(self.sem, 1)
        self.n += 1

    def wait(self):
        self.eng.wait_ge(self.sem, self.base + self.n)

    def enter(self, it, per):
        self.start = self.base + self.n
        self.base, self.n, self.per = it * per + self.start, 0, per

    def leave(self, times):
        assert self.n == self.per, (self.n, self.per)
        self.base, self.n = self.start + times * self.per, 0


def build(nc, A, O):
    base = (nc.sbuf_base + 31) // 32 * 32
    end = 229344

    def place(name, shape, dt, off):
        n = int(np.prod(shape[1:])) * 4
        assert base + off + n <= end, (name, base + off + n - end)
        return nc.alloc_sbuf_tensor_at(name, shape, dt, offset=base + off), off + (n + 31) // 32 * 32

    o = 0
    XH, o = place("x_high", [P, KT, T], F32R, o)
    XL, o = place("x_low", [P, KT, T], F32R, o)
    o_hb = o
    HB, o = place("residual", [P, KT * T], F32, o)
    RAW, WH, WL = [None, None], [None, None], [None, None]
    for s in range(2):
        RAW[s], o = place(f"w_raw{s}", [P, UNIT], F32, o)
        WH[s], o = place(f"w_high{s}", [P, UNIT], F32R, o)
        WL[s], o = place(f"w_low{s}", [P, UNIT], F32R, o)
    o_za = o
    ZA, o = place("gate_rank", [RANK, T], F32, o)
    ACC, _ = place("square_sum", [P, T], F32, o_za)
    RN, o = place("inv_rms", [P, T], F32, o)
    IDENT, o = place("ident", [P, P], F32, o)
    ONES, o = place("ones", [P, P], F32, o)
    GA, o = place("g_attn", [P, KT], F32, o)
    GF, o = place("g_ffn", [P, KT], F32, o)
    GZ, o = place("g_final", [P, KT], F32, o)
    GG, o = place("g_gla", [P, 2 * GH], F32, o)
    BG, o = place("b_gate", [P, GH], F32, o)
    SM, o = place("stats", [P, 24], F32, o)
    o_scr = o

    GRP, o = place("proj", [P, 2, 3, T], F32, o_scr)
    o_att = o
    VN, o = place("v_rows", [P, 5, HD], F32, o)
    KNEW, o = place("k_new_rows", [SAMP, HD], F32, o)
    SP_, o = place("probs", [P, 1280], F32, o)
    o_pt = o
    PT, o = place("probs_t", [P, 4, SEQ], F32, o)
    TABP, o = place("bias_prompt", [P, SEQ], F32, o)
    TABS, o = place("bias_sample", [SAMP, NKEY], F32, o)
    o_kt = o
    KTH, o = place("k_t_high", [P, NKEY - SAMP], F32R, o)
    KTL, o = place("k_t_low", [P, NKEY - SAMP], F32R, o)
    SS, o = place("probs_sample", [SAMP, NKEY], F32, o)
    PTS, o = place("probs_sample_t", [P, 9, SAMP], F32, o)
    QP, o = place("q_padded", [P, NB * (2 * SAMP + NQ)], F32R, o)
    OT, o = place("mixed_rows", [P, 2, P], F32, o)
    KR, VR = [None, None], [None] * 4
    VR[2], r = place("v_cache_rows2", [P, 8, HD], F32, o_pt)
    VR[3], r = place("v_cache_rows3", [P, 8, HD], F32, r)
    assert r - o_pt <= 4 * SEQ * 4
    r = o_hb
    for s in range(2):
        KR[s], r = place(f"k_rows{s}", [P, 8, HD], F32, r)
        VR[s], r = place(f"v_cache_rows{s}", [P, 8, HD], F32, r)
    assert r - o_hb <= 8 * T * 4
    o = o_kt
    ZRAW, o = place("za_raw", [P, KT, RANK], F32, o)
    ZH, o = place("za_high", [P, KT, RANK], F32R, o)
    ZL, o = place("za_low", [P, KT, RANK], F32R, o)

    o = o_att
    QD, o = place("q_decayed", [P, T], F32, o)
    KD, o = place("k_decayed", [P, T], F32, o)
    EA, o = place("tmp_a", [P, T], F32, o)
    EB, o = place("tmp_b", [P, T], F32, o)
    o_la = o
    KN, o = place("k_to_end_rows", [P, 5, DK], F32, o)
    LA, _ = place("log_decay", [P, T], F32, o_la)
    GVN, o = place("gla_v_rows", [P, 5, DV], F32, o)
    ST, o = place("states", [P, NCH, DV], F32, o)
    S0, o = place("states_sample", [P, NB, DV], F32, o)
    VM, o = place("v_masked", [SAMP, 4, DV], F32, o)
    RESET, o = place("chunk_starts", [P, T], F32, o)
    PM, o = place("causal_pair", [P, P], F32, o)
    SMK, o = place("causal_sample", [SAMP, SAMP], F32, o)
    RM, o = place("row_of_sample", [SAMP, NB], F32, o)
    WG, o = place("w_gate", [RANK, DK], F32, o)
    ET, o = place("decay_total", [P, 16], F32, o)
    AT = KD

    o = o_scr
    AH, AL = [None, None], [None, None]
    for s in range(2):
        AH[s], o = place(f"act_high{s}", [P, GT, T], F32R, o)
        AL[s], o = place(f"act_low{s}", [P, GT, T], F32R, o)
    UW = 2 + SEQ + NB * 6
    CW = UW - 2
    UA, o = place("u_gate", [P, UW], F32, o)
    UV, o = place("u_value", [P, UW], F32, o)
    o_c = o
    CA, o = place("conv_gate", [P, CW], F32, o)
    CV, o = place("conv_value", [P, CW], F32, o)
    XR = [None, None]
    XR[0], o2 = place("x_again0", [P, T], F32, o_c)
    XR[1], o2 = place("x_again1", [P, T], F32, o2)
    assert o2 <= o
    SQ, o = place("squares", [P, T], F32, o)
    PR = SQ
    WC, o = place("w_conv", [P, 3, 2 * FT], F32, o)
    BC, o = place("b_conv", [P, 2 * FT], F32, o)
    CI = [None, None]
    CI[0], o = place("conv_in0", [P, 2, GT, 16], F32, o)
    CI[1], o = place("conv_in1", [P, 2, GT, 16], F32, o)
    CO = [None, None]
    CO[0], o = place("conv_out0", [P, 2, GT, 18], F32, o)
    CO[1], o = place("conv_out1", [P, 2, GT, 18], F32, o)

    bank = [nc.alloc_psum_tensor(n, [P, 512], F32) for n in ("bSA", "bSB", "bO", "bZ", "bT0", "bT1", "bPA", "bPB")]
    SA, SB, BO, BZ, T0, T1, PA, PB = bank
    PJ = [PA, PB]

    def sem(name):
        return nc.alloc_semaphore(name)

    raw_ready = [sem("raw_ready0"), sem("raw_ready1")]
    x_in, consts_in, za_in = [sem(f"x_in{i}") for i in range(4)], sem("consts_in"), sem("za_in")
    hi_done, lo_done = sem("hi_done"), sem("lo_done")
    xh_done, xl_done, sq_done = sem("xh_done"), sem("xl_done"), sem("sq_done")
    zs_done = sem("zs_done")
    sums_done, ms_done, sqrt_done, rn_done = sem("sums_done"), sem("ms_done"), sem("sqrt_done"), sem("rn_done")
    za_half, za_done = sem("za_half"), sem("za_done")
    half_done, half_read = sem("half_done"), sem("half_read")
    v_turned, v_rows_done = sem("v_turned"), sem("v_rows_done")
    scores_done, max_done, exp_done, norm_done = sem("scores_done"), sem("max_done"), sem("exp_done"), sem("norm_done")
    probs_turned, pt_done = sem("probs_turned"), sem("pt_done")
    k_in, vnear_in, vfar_in = [sem("k_in0"), sem("k_in1")], [sem(f"vnear_in{i}") for i in range(4)], [sem(f"vfar_in{i}") for i in range(4)]
    rows_free, state_free = sem("rows_free"), sem("state_free")
    k_turned, kh_done, kl_done = sem("k_turned"), sem("kh_done"), sem("kl_done")
    qk_done, qp_done, qp_high = sem("qk_done"), sem("qp_done"), sem("qp_high")
    smax_done, sexp_done, snorm_done = sem("smax_done"), sem("sexp_done"), sem("snorm_done")
    sprobs_turned, pts_done = sem("sprobs_turned"), sem("pts_done")
    pv_done, pv_read, pvs_done, pvs_read = sem("pv_done"), sem("pv_read"), sem("pvs_done"), sem("pvs_read")
    ot_done, ot_turned = sem("ot_done"), sem("ot_turned")
    tabp_in, tabs_in, head_stored = sem("tabp_in"), sem("tabs_in"), sem("head_stored")
    qp_zero = sem("qp_zero")
    scratch_free, gconst_in, wg_in, s0_in = sem("scratch_free"), sem("gconst_in"), sem("wg_in"), sem("s0_in")
    z_done, z_read, e_done = sem("z_done"), sem("z_read"), sem("e_done")
    qd_done, kd_done, ke_done, dt_done, la_done = sem("qd_done"), sem("kd_done"), sem("ke_done"), sem("dt_done"), sem("la_done")
    gv_turned, gv_done = sem("gv_turned"), sem("gv_done")
    at_done, at_read, kn_turned, kn_done = sem("at_done"), sem("at_read"), sem("kn_turned"), sem("kn_done")
    inc_done, state_done, o_done, sqg_done = sem("inc_done"), sem("state_done"), sem("o_done"), sem("sqg_done")
    vm_done, us_done, ss_done = sem("vm_done"), sem("us_done"), sem("ss_done")
    sq2_done, gsum_done, gms_done, gsqrt_done = sem("sq2_done"), sem("gsum_done"), sem("gms_done"), sem("gsqrt_done")
    silu_done, mix_done, state_stored, sstate_stored = sem("silu_done"), sem("mix_done"), sem("state_stored"), sem("sstate_stored")
    mh_done, ml_done, xr_in = sem("mh_done"), sem("ml_done"), [sem("xr_in0"), sem("xr_in1")]
    hsq_done, acc_done = sem("hsq_done"), sem("acc_done")
    fh_done, fl_done = sem("fh_done"), sem("fl_done")
    fhalf_done, fhalf_read = sem("fhalf_done"), sem("fhalf_read")
    ci_in, co_ready, co_stored, conv_in = [sem("ci_in0"), sem("ci_in1")], sem("co_ready"), sem("co_stored"), sem("conv_in")
    aff_done, conv_done, silu2_done, prod_done = sem("aff_done"), sem("conv_done"), sem("silu2_done"), sem("prod_done")
    ah_done, al_done = sem("ah_done"), sem("al_done")
    y_done, out_stored, copied = sem("y_done"), sem("out_stored"), sem("copied")
    passed = sem("passed")
    act_own, dve_own, pool_own = sem("act_own"), sem("dve_own"), sem("pool_own")

    def w_cols(w, col):
        return w.rearrange("(k p) n -> p k n", p=P)[:, :, bass.ds(col, P) if not isinstance(col, int) else slice(col, col + P)]

    def raw3(s):
        return RAW[s][:, :].rearrange("p (k n) -> p k n", k=KT)

    def raw4(s):
        return RAW[s][:, :].rearrange("p (k n) -> p k n", k=GT)

    def hb(tile, lo=0, n=T):
        start = tile * T + lo
        return HB[:, start:start + n] if isinstance(tile, int) else HB[:, bass.ds(start, n)]

    def samples(ap):
        return ap.rearrange("p (b i) -> p b i", i=NQ)

    def addition(ch):
        j = (ch // 2) % 2
        return [T0, T1, BO, BZ][2 * (ch % 2) + ch // 4][:, j * DV:(j + 1) * DV]

    POFF = [0, 128, 384, 768]
    block = nc.Block()
    block.__enter__()

    @block.sync
    def _(sp):
        def load_unit(src, dst, c, it=None, k=0):
            if c >= 2:
                sp.wait_ge(lo_done, at(c - 1, it, k))
            sp.dma_start(dst(c % 2), src).then_inc(raw_ready[c % 2], 16)

        def copy_cache(kv, b, j):
            name = "cache_swa_k" if kv == 0 else "cache_swa_v"
            oname = "k_sample" if kv == 0 else "v_sample"
            n = CHUNK_ROWS * HEADS * HD
            row = HEADS * HD

            def flat(ap, first):
                v = ap.rearrange("b r h d -> b (r h d)")
                v = v[b:b + 1] if isinstance(b, int) else v[bass.ds(b, 1)]
                lo = first * row
                return v[:, lo:lo + n].rearrange("b (s m) -> (b s) m", s=16)
            sp.dma_start(flat(O[oname], j * CHUNK_ROWS), flat(A[name], NQ + j * CHUNK_ROWS)).then_inc(copied, 16)

        def head_of(ap, b, r0, n, h, pat, **kw):
            v = ap[b, r0:r0 + n]
            v = v[:, h:h + 1, :] if isinstance(h, int) else v[:, bass.ds(h, 1), :]
            return v.rearrange(pat, **kw)

        def load_near(name, dst, b, h, s):
            near = head_of(A[name], b, PAST - NEAR, NEAR, h, "(p j) h d -> p j (h d)", j=4)
            sp.dma_start(dst[:, 0:4, :], near).then_inc(s, 16)

        def load_far(name, dst, b, h, s):
            far = head_of(A[name], b, 0, PAST - NEAR, h, "(a r) h d -> a r (h d)", r=16)[:, 0:4, :]
            sp.dma_start(dst[0:FAR, 4:8, :], far).then_inc(s, 16)

        for i in range(4):
            sp.dma_start(HB[:, :].rearrange("p (k t) -> p k t", k=KT)[:, 4 * i:4 * i + 4, :],
                         A["x_t"][:, 4 * i:4 * i + 4, :]).then_inc(x_in[i], 16)
            if i == 0:
                for dst, name in ((GA, "g_attn"), (ONES, "ones"), (IDENT, "ident"), (GF, "g_ffn"), (GZ, "g_final"),
                                  (GG, "g_gla"), (BG, "b_gate")):
                    sp.dma_start(dst[:, :], A[name]).then_inc(consts_in, 16)
                sp.dma_start(ZRAW[:, :, :], A["w_in"].rearrange("(k p) n -> p k n", p=P)[:, :, C_ZA:C_ZA + RANK]).then_inc(za_in, 16)
        w_in = A["w_in"]
        for c, col in enumerate((C_QB, C_KB, C_VB, C_QB + P, C_KB + P, C_VB + P)):
            load_unit(w_cols(w_in, col), raw3, c)
        sp.wait_ge(sums_done, 2)

        def swa_loads(h, hc, it, cols, copies):
            def k_rows(b):
                n = 8 * hc + b - 1
                if n > 0:
                    sp.wait_ge(k_turned, at(n, it, 16))
                load_near("cache_swa_k", KR[b % 2], b, h, k_in[b % 2])
                load_far("cache_swa_k", KR[b % 2], b, h, k_in[b % 2])

            def v_rows(b):
                n = 16 * hc + 2 * (b - 4)
                if b in (2, 3):
                    sp.wait_ge(pv_done, at(hc + 1, it, 2))
                for i, load in enumerate((load_near, load_far)):
                    if n >= 0 and b not in (2, 3):
                        sp.wait_ge(pvs_done, at(n + i + 1, it, 32))
                    load("cache_swa_v", VR[b % 4], b, h, [vnear_in, vfar_in][i][b % 4])
            u = 3 * hc + 6
            k_rows(0)
            k_rows(1)
            v_rows(0)
            v_rows(1)
            load_unit(w_cols(w_in, cols[0]), raw3, u, it, 6)
            copies(0)
            k_rows(2)
            copies(1)
            v_rows(2)
            k_rows(3)
            load_unit(w_cols(w_in, cols[1]), raw3, u + 1, it, 6)
            copies(2)
            v_rows(3)
            for b in range(4, NB):
                k_rows(b)
                copies(b - 1)
            for b in range(4, NB):
                v_rows(b)
            load_unit(w_cols(w_in, cols[2]), raw3, u + 2, it, 6)

        def next_cols(h):
            return [C_QB + P * (h + 2), C_KB + P * (h + 2), C_VB + P * (h + 2)]
        for h in range(2):
            swa_loads(h, h, None, next_cols(h), lambda i: None)
        with sp.Fori(0, 2) as it:
            for hh in range(2):
                def copies(i, hh=hh):
                    copy_cache(0, it, 7 * hh + i)
                h = it * 2 + (2 + hh)
                swa_loads(h, 2 + hh, it, [h * P + (C_QB + 2 * P), h * P + (C_KB + 2 * P), h * P + (C_VB + 2 * P)], copies)
        swa_loads(6, 6, None, [C_QA, C_KA, C_VA], lambda i: None)
        swa_loads(7, 7, None, [C_VA + P, C_GA, C_GA + P], lambda i: [copy_cache(0, 2, 2 * i + j) for j in range(2)])

        with sp.Fori(0, GH - 1) as it:
            cols = [it * P + (C_QA + P), it * P + (C_KA + P), it * DV + (C_VA + DV),
                    it * DV + (C_VA + DV + P), it * DV + (C_GA + DV), it * DV + (C_GA + DV + P)]
            j = 0
            for i, col in enumerate(cols):
                load_unit(w_cols(w_in, col), raw3, U_GLA + 6 + i, it, 6)
                for _ in range(3 if i < 2 else 2):
                    copy_cache(1, it, j)
                    j += 1
            assert j == COPIES
        w_out = A["w_out"]
        for m in range(3):
            load_unit(w_cols(w_out, m * P), raw3, U_OUT + m)

        def load_x(m, mc, it=None):
            if mc >= 2:
                sp.wait_ge(half_read, at(2 * (U_OUT + mc - 2) + 2, it, 8))
            sp.dma_start(XR[mc % 2][:, :], A["x_t"][:, bass.ds(m, 1), :].rearrange("p o t -> p (o t)")
                         if it is not None else A["x_t"][:, m, :]).then_inc(xr_in[mc % 2], 16)
        sp.wait_ge(mix_done, 2 * GH)
        sp.wait_ge(state_stored, 16 * GH)
        sp.wait_ge(sstate_stored, 16 * GH)
        sp.dma_start(WC[:, :, :], A["w_conv"]).then_inc(conv_in, 16)
        sp.dma_start(BC[:, :], A["b_conv"]).then_inc(conv_in, 16)
        load_x(0, 0)
        load_x(1, 1)
        with sp.Fori(0, 3) as it:
            for i in range(4):
                load_unit(w_cols(w_out, it * 4 * P + (3 + i) * P), raw3, U_OUT + 3 + i, it, 4)
                load_x(it * 4 + (2 + i), 2 + i, it)
        load_unit(w_cols(w_out, 15 * P), raw3, U_OUT + 15)
        load_x(14, 14)
        load_x(15, 15)

        w_up, w_down = A["w_up"], A["w_down"].rearrange("(n k p) m -> n p k m", k=GT, p=P)
        cin = A["conv_in"].rearrange("p (s n) x -> p s n x", s=2)

        def up_units(g, c, it=None, k=0, after=None):
            for j in range(GT):
                for s in range(2):
                    col = (s * FT + j) * P
                    col = g * (GT * P) + col
                    load_unit(w_cols(w_up, col), raw3, c + 2 * j + s, it, k)
                    if after:
                        after(2 * j + s)

        def down_units(g, c, it=None, k=0, after=None):
            for m in range(DOWN):
                src = w_down[g] if isinstance(g, int) else w_down[bass.ds(g, 1)].rearrange("o p k m -> (o p) k m")
                load_unit(src[:, :, m * 512:(m + 1) * 512], raw4, c + m, it, k)
                if after:
                    after(PAIR + m)

        sp.dma_start(CI[0][:, :, :, :], cin[:, :, 0:GT, :]).then_inc(ci_in[0], 16)
        up_units(0, U_FFN)
        with sp.Fori(0, (NG - 1) // 2) as it:
            for p in range(2):
                c = U_FFN + PAIR + p * (PAIR + DOWN)

                def after(k, p=p):
                    n = p * (PAIR + DOWN) + k
                    if n < COPIES:
                        copy_cache(0, it + 3, n)
                    if n >= 2 * (PAIR + DOWN) - COPIES:
                        copy_cache(1, it + 3, n - (2 * (PAIR + DOWN) - COPIES))
                g = it * 2 + (1 + p)
                sp.wait_ge(conv_done, it * (2 * PAIR) + (PAIR if p else 1))
                sp.dma_start(CI[(1 + p) % 2][:, :, :, :], cin[:, :, bass.ds(g * GT, GT), :]).then_inc(ci_in[(1 + p) % 2], 16)
                up_units(g, c, it, 2 * (PAIR + DOWN), after)
                down_units(it * 2 + p, c + PAIR, it, 2 * (PAIR + DOWN), after)
        down_units(NG - 1, U_FFN + NG * PAIR + (NG - 1) * DOWN)
        for i in range(4):
            sp.wait_ge(y_done, 4 * i + 4)
            sp.dma_start(O["y_t"][:, 4 * i:4 * i + 4, :],
                         HB[:, 4 * i * T:(4 * i + 4) * T].rearrange("p (k t) -> p k t", k=4)).then_inc(out_stored, 16)
        sp.wait_ge(out_stored, 16 * 4)
        sp.wait_ge(copied, 16 * 2 * NB * COPIES)

    @block.tensor
    def _(pe):
        def mm3(out, w_h, w_l, x_h, x_l, first, last):
            pe.matmul(out, w_h, x_h, start=first, stop=False)
            pe.matmul(out, w_h, x_l, start=False, stop=False)
            return pe.matmul(out, w_l, x_h, start=False, stop=last)

        def sums(src):
            for x in range(2):
                ins = pe.matmul(PJ[x][:, 0:HALF], ONES[:, :], src[:, x * HALF:(x + 1) * HALF], start=True, stop=True)
                ins.then_inc(sums_done, 1)

        def steps(x, c, lo, hi, it=None, k=0):
            if lo == 0 and x == 0:
                pe.wait_ge(lo_done, at(c + 1, it, k))
            if lo == 0 and c >= 1:
                pe.wait_ge(half_read, at(2 * c + x - 1, it, 2 * k))
            s = c % 2
            order = [*range(KT)] if c < U_OUT else [*range(8, KT), *range(8)]
            for n in range(lo, hi):
                kt = order[n]
                if c == U_OUT and it is None and x == 0:
                    pe.wait_ge(ml_done, n + 1)
                w = slice(kt * P, (kt + 1) * P)
                t = slice(x * HALF, (x + 1) * HALF)
                ins = mm3(PJ[x][:, 0:HALF], WH[s][:, w], WL[s][:, w], XH[:, kt, t], XL[:, kt, t], n == 0, n == KT - 1)
            if hi == KT:
                ins.then_inc(half_done, 1)

        def project(x, c, it=None, k=0):
            steps(x, c, 0, KT, it, k)

        def part(u, lo, hi, it, k):
            while lo < hi:
                x, n = (lo // KT) % 2, lo % KT
                end = min(KT, n + hi - lo)
                steps(x, u + lo // (2 * KT), n, end, it, k)
                lo += end - n

        def turn(out, in_, n):
            return pe.transpose(out, in_, IDENT[0:n, 0:n])

        pe.wait_ge(consts_in, 16 * 7)
        for k in range(KT):
            pe.wait_ge(sq_done, k + 1)
            for x in range(2):
                ins = pe.matmul(PJ[x][:, 0:HALF], ONES[:, :], hb(k, x * HALF, HALF), start=k == 0, stop=k == KT - 1)
                if k == KT - 1:
                    ins.then_inc(sums_done, 1)
        pe.wait_ge(zs_done, 2)
        for x in range(2):
            for k in range(KT):
                t = slice(x * HALF, (x + 1) * HALF)
                ins = mm3([SA, SB][x][0:P, 0:HALF][0:RANK], ZH[:, k, :], ZL[:, k, :], XH[:, k, t], XL[:, k, t], k == 0, k == KT - 1)
            ins.then_inc(za_half, 1)
        pe.wait_ge(ms_done, 2)
        for u in range(3):
            project(0, u)
            project(1, u)

        def swa_head(hc, it):
            def n(per, c):
                return at(per * hc + c, it, 2 * per)
            g = GRP[:, hc % 2]
            q, k, v = g[:, 0], g[:, 1], g[:, 2]
            u = 3 * hc + 3
            pe.wait_ge(half_read, n(6, 6))
            for j in range(4):
                turn(T0[:, j * P:(j + 1) * P], v[:, j * P:(j + 1) * P], P)
            turn(T1[0:SAMP, 0:HD], v[:, SEQ:T], P)
            turn(T1[0:SAMP, HD:2 * HD], k[:, SEQ:T], P).then_inc(v_turned, 1)
            part(u, 0, 16, it, 6)
            pe.wait_ge(v_rows_done, n(3, 3))
            pe.wait_ge(half_read, at(2 * u + 1, it, 12))
            for i in range(4):
                pe.matmul([SA, SB, BO, BZ][i][:, 0:(i + 1) * P], q[:, i * P:(i + 1) * P], k[:, 0:(i + 1) * P],
                          start=True, stop=True).then_inc(scores_done, 1)
            part(u, 16, 32, it, 6)
            pe.wait_ge(norm_done, n(4, 4))
            for i in range(4):
                for j in range(i + 1):
                    dst = [SA[:, 0:P], SA[:, P:3 * P], SB[:, 0:3 * P], BO[:, :]][i]
                    ins = turn(dst[:, j * P:(j + 1) * P], SP_[:, POFF[i] + j * P:POFF[i] + (j + 1) * P], P)
            ins.then_inc(probs_turned, 1)

            def turn_keys(b):
                pe.wait_ge(k_in[b % 2], at(32 * (4 * hc + b // 2 + 1), it, 32 * 8))
                for j in range(4):
                    turn(T0[:, j * P:(j + 1) * P], KR[b % 2][:, j, :], P)
                for j in range(4):
                    ins = turn(T1[:, j * FAR:(j + 1) * FAR], KR[b % 2][0:FAR, 4 + j, :], FAR)
                ins.then_inc(k_turned, 1)
            turn_keys(0)
            part(u, 32, 40, it, 6)
            pe.wait_ge(pt_done, n(4, 4))
            for j in range(4):
                ins = pe.matmul(BZ[:, j * P:SEQ], VN[:, j, :], PT[:, j, j * P:SEQ], start=j == 0, stop=j == 3, skip_group_check=True)
            ins.then_inc(pv_done, 1)
            pe.wait_ge(qp_done, n(1, 1))
            for b in range(NB):
                pe.wait_ge(kl_done, n(16, 2 * b + 2))
                both = QP[:, b * 2 * SAMP:(b + 1) * 2 * SAMP]
                high = QP[:, b * 2 * SAMP:b * 2 * SAMP + SAMP]
                for dst, w, rows, cols in ((SA, KTH, both, slice(0, NEAR)), (SB, KTH, both, slice(NEAR, NKEY - SAMP)),
                                           (SA, KTL, high, slice(0, NEAR)), (SB, KTL, high, slice(NEAR, NKEY - SAMP))):
                    m = rows.shape[1]
                    ins = pe.matmul(dst[0:m, 0:cols.stop - cols.start], rows, w[:, cols], start=b == 0 and m > SAMP,
                                    stop=b == NB - 1 and m == SAMP, skip_group_check=True)
                if b == 0:
                    pe.matmul(SB[0:SAMP, 4 * FAR:4 * FAR + SAMP], q[:, SEQ:T], k[:, SEQ:T], start=False, stop=True, skip_group_check=True)
                if b + 1 < NB:
                    turn_keys(b + 1)
                    part(u, 40 + 5 * b, 45 + 5 * b, it, 6)
            ins.then_inc(qk_done, 1)
            part(u, 75, 84, it, 6)
            pe.wait_ge(snorm_done, n(1, 1))
            pe.sem_inc(passed, 1)
            for j in range(4):
                turn(T0[:, j * SAMP:(j + 1) * SAMP], SS[:, j * P:(j + 1) * P], SAMP)
            for j in range(4):
                turn(T0[0:FAR, (4 + j) * SAMP:(5 + j) * SAMP], SS[:, NEAR + j * FAR:NEAR + (j + 1) * FAR], SAMP)
            turn(T0[0:SAMP, 8 * SAMP:9 * SAMP], SS[:, NEAR + 4 * FAR:NKEY], SAMP).then_inc(sprobs_turned, 1)
            part(u, 84, 88, it, 6)
            pe.wait_ge(pts_done, n(3, 3))
            pe.wait_ge(pv_read, n(1, 1))
            for b in range(NB):
                out = BZ[b % 4 * SAMP:(b % 4 + 1) * SAMP, b // 4 * P:(b // 4 + 1) * P]
                for j in range(8):
                    if j % 4 == 0:
                        pe.wait_ge([vnear_in, vfar_in][j // 4][b % 4], at(16 * (2 * hc + b // 4 + 1), it, 16 * 4))
                    rows = P if j < 4 else FAR
                    ins = pe.matmul(out, PTS[0:rows, j, :], VR[b % 4][0:rows, j, :], start=j == 0, stop=j == 7, skip_group_check=True)
                    if j % 4 == 3:
                        ins.then_inc(pvs_done, 1)
                if b in (3, 5):
                    part(u, 88 + b - 3, 90 + b - 3, it, 6)
            part(u, 92, 96, it, 6)
            pe.matmul(BO[:, 0:SAMP], VN[0:SAMP, 4, :], PTS[0:SAMP, 8, :], start=True, stop=True)
            pe.wait_ge(ot_done, n(1, 1))
            for w in range(2):
                ins = turn(BO[:, (w + 1) * P:(w + 2) * P], OT[:, w, :], P)
            ins.then_inc(ot_turned, 1)
        with pe.Fori(0, HEADS // 2) as it:
            for hh in range(2):
                swa_head(hh, it)

        def gla_head(it, c, last):
            def n(per, d):
                return at(per * c + d, it, per)
            u = U_GLA + 3 + 6 * c
            g0, g1 = GRP[:, 0], GRP[:, 1]
            pe.wait_ge(wg_in, n(16, 16))
            pe.wait_ge(za_done, 2)
            pe.wait_ge(half_read, at(2 * u, it, 12))
            pe.matmul(T0[:, 0:SEQ], WG[:, :], ZA[:, 0:SEQ], start=True, stop=True)
            pe.matmul(T1[:, 0:SAMP], WG[:, :], ZA[:, SEQ:T], start=True, stop=True).then_inc(z_done, 1)
            project(0, u, it, 6)
            project(1, u, it, 6)

            def turn_v(src):
                for j in range(4):
                    turn(BO[:, j * P:(j + 1) * P], src[:, j * P:(j + 1) * P], P)
                turn(T1[0:SAMP, 0:P], src[:, SEQ:T], P).then_inc(gv_turned, 1)
            pe.wait_ge(z_read, n(2, 2))
            turn_v(g0[:, 2])
            project(0, u + 1, it, 6)
            pe.wait_ge(kd_done, n(1, 1))
            pe.wait_ge(qd_done, n(1, 1))
            for j in range(4):
                t = slice(j * P, (j + 1) * P)
                pe.matmul(SA[:, t], KD[:, t], QD[:, t], start=True, stop=True)
            pe.matmul(SB[0:SAMP, 0:SAMP], KD[:, SEQ:T], QD[:, SEQ:T], start=True, stop=True).then_inc(at_done, 1)
            pe.wait_ge(ke_done, n(1, 1))
            pe.wait_ge(gv_done, n(4, 2))
            for j in range(4):
                turn(T0[:, j * P:(j + 1) * P], g0[:, 1, j * P:(j + 1) * P], P)
            turn(T1[0:SAMP, 0:P], g0[:, 1, SEQ:T], P).then_inc(kn_turned, 1)
            project(1, u + 1, it, 6)
            pe.wait_ge(kn_done, n(2, 2))
            pe.wait_ge(half_read, at(2 * u + 2, it, 12))
            turn_v(g1[:, 0])
            project(0, u + 2, it, 6)
            pe.wait_ge(gv_done, n(4, 4))
            for ch in range(NCH):
                rows = slice((ch % 2) * CH, (ch % 2 + 1) * CH)
                ins = pe.matmul(addition(ch), KN[rows, ch // 2, :], GVN[rows, ch // 2, :],
                                start=True, stop=True)
            ins.then_inc(inc_done, 1)
            project(1, u + 2, it, 6)
            if not last:
                project(0, u + 3, it, 6)
            pe.wait_ge(at_read, n(2, 2))
            pe.wait_ge(state_done, n(8, 8))
            for w in range(2):
                o_ = [SA, SB][w]
                dv = slice(w * P, (w + 1) * P)
                for j in range(4):
                    t = slice(j * P, (j + 1) * P)
                    pe.matmul(o_[:, t], GVN[:, j, dv], AT[:, t], start=j == 0, stop=True, skip_group_check=True)
                for ch in range(1, NCH):
                    t = slice(ch * CH, (ch + 1) * CH)
                    pe.matmul(o_[:, t], ST[:, ch - 1, dv], QD[:, t], start=False, stop=True, skip_group_check=True)
            pe.wait_ge(s0_in, n(16, 16))
            for w in range(2):
                dv = slice(w * P, (w + 1) * P)
                o_ = T0[:, w * SAMP:(w + 1) * SAMP]
                pe.matmul(o_, GVN[0:SAMP, 4, dv], AT[0:SAMP, SEQ:T], start=w == 0, stop=True, skip_group_check=True)
                for b in range(NB):
                    cols = slice(b * NQ, (b + 1) * NQ)
                    ins = pe.matmul(o_[:, cols], S0[:, b, dv], QD[:, SEQ + b * NQ:SEQ + (b + 1) * NQ], start=False, stop=True, skip_group_check=True)
            ins.then_inc(o_done, 1)
            if not last:
                project(1, u + 3, it, 6)

            def sample_adds(i):
                pe.wait_ge(vm_done, n(2, i + 1))
                for b in range(4):
                    dst = [T1, BO][b // 2]
                    ins = pe.matmul(dst[:, (b % 2) * DV:(b % 2 + 1) * DV], KN[0:SAMP, 4, :], VM[:, b, :], start=True, stop=True)
                ins.then_inc(us_done, 1)
            sample_adds(0)
            pe.wait_ge(sq2_done, n(1, 1))
            pe.matmul(BZ[:, 0:SEQ], ONES[:, :], EA[:, 0:SEQ], start=True, stop=True)
            pe.wait_ge(ss_done, n(2, 1))
            pe.matmul(T1[:, 0:SAMP], ONES[:, :], EA[:, SEQ:T], start=True, stop=True).then_inc(gsum_done, 1)
            if not last:
                project(0, u + 4, it, 6)
            pe.wait_ge(gms_done, n(2, 2))
            sample_adds(1)
            if not last:
                project(1, u + 4, it, 6)
                project(0, u + 5, it, 6)
                project(1, u + 5, it, 6)
        with pe.Fori(0, GH - 1) as it:
            gla_head(it, 0, False)
        gla_head(None, GH - 1, True)

        project(0, U_OUT)
        project(1, U_OUT)
        project(0, U_OUT + 1)
        project(1, U_OUT + 1)
        with pe.Fori(0, 7) as it:
            for i in range(2):
                project(0, U_OUT + 2 + i, it, 2)
                project(1, U_OUT + 2 + i, it, 2)

        def up(c, f, it=None, first=False):
            for x in range(2):
                n = f + x
                if x == 0:
                    pe.wait_ge(lo_done, at(c + 1, it, 24))
                if n >= 8:
                    pe.wait_ge(fhalf_read, at(n - 7, it, 96))
                s = c % 2
                for kt in range(KT):
                    if first and x == 0:
                        pe.wait_ge(fl_done, kt + 1)
                    w = slice(kt * P, (kt + 1) * P)
                    t = slice(x * HALF, (x + 1) * HALF)
                    ins = mm3(bank[n % 8][:, 0:HALF], WH[s][:, w], WL[s][:, w], XH[:, kt, t], XL[:, kt, t], kt == 0, kt == KT - 1)
                ins.then_inc(fhalf_done, 1)
                if first and x == 0:
                    pe.wait_ge(acc_done, KT)
                    sums(ACC)

        def down(c, f, gpar, acts, it=None):
            pe.wait_ge(lo_done, at(c + 1, it, 24))
            pe.wait_ge(al_done, at(acts, it, 2 * GT))
            s = c % 2
            for j in range(4):
                for x in range(2):
                    n = f + 2 * j + x
                    pe.wait_ge(fhalf_read, at(n - 7, it, 96))
                    for kt in range(GT):
                        w = slice(kt * 512 + j * P, kt * 512 + (j + 1) * P)
                        t = slice(x * HALF, (x + 1) * HALF)
                        ins = mm3(bank[n % 8][:, 0:HALF], WH[s][:, w], WL[s][:, w], AH[gpar][:, kt, t], AL[gpar][:, kt, t], kt == 0, kt == GT - 1)
                    ins.then_inc(fhalf_done, 1)
        for i in range(PAIR):
            up(U_FFN + i, 2 * i, None, i == 0)
        c0, f0 = U_FFN + PAIR, 2 * PAIR
        with pe.Fori(0, (NG - 1) // 2) as it:
            for p in range(2):
                c, f = c0 + p * (PAIR + DOWN), f0 + p * 48
                for i in range(PAIR):
                    up(c + i, f + 2 * i, it)
                for i in range(DOWN):
                    down(c + PAIR + i, f + 16 + 8 * i, p, GT * (p + 1), it)
        c, f = U_FFN + NG * PAIR + (NG - 1) * DOWN, f0 + (NG - 1) * 48
        for i in range(DOWN):
            down(c + i, f + 8 * i, 0, GT * NG)
        pe.wait_ge(acc_done, 2 * KT)
        pe.wait_ge(fhalf_read, f + 8 * DOWN)
        sums(ACC)

    @block.scalar
    def _(act):
        own = Order(act, act_own)

        def hi(c, it=None, k=0, ffn=None):
            act.wait_ge(raw_ready[c % 2], at(16 * (c // 2 + 1), it, 8 * k))
            if ffn is not None:
                act.wait_ge(fhalf_done, at(ffn, it, 96))
            elif c >= 2:
                act.wait_ge(half_done, at(2 * c - 2, it, 2 * k))
            act.activation(WH[c % 2][:, :], RAW[c % 2][:, :], ACT.Copy).then_inc(hi_done, 1)

        act.wait_ge(consts_in, 16 * 7)
        for k in range(KT):
            act.wait_ge(x_in[k // 4], 16)
            act.activation(XH[:, k, :], hb(k), ACT.Copy, scale=GA[:, k:k + 1]).then_inc(xh_done, 1)
        act.wait_ge(za_in, 16)
        act.activation(ZH[:, :, :], ZRAW[:, :, :], ACT.Copy).then_inc(zs_done, 1)
        for k in range(KT):
            act.wait_ge(xl_done, k + 1)
            act.activation(hb(k), hb(k), ACT.Square).then_inc(sq_done, 1)
        hi(0)
        hi(1)
        act.wait_ge(ms_done, 2)
        act.activation(RN[:, :], RN[:, :], ACT.Sqrt).then_inc(sqrt_done, 1)
        hi(2)
        hi(3)

        def swa_head(hc, it):
            def n(per, c):
                return at(per * hc + c, it, 2 * per)
            u = 3 * hc + 3
            hi(u + 1, it, 6)
            act.wait_ge(v_turned, n(1, 1))
            act.wait_ge(rows_free, n(1, 1))
            act.activation(VN[:, 0:4, :], T0[:, :].rearrange("p (j d) -> p j d", j=4), ACT.Copy).then_inc(v_rows_done, 1)
            act.activation(VN[0:SAMP, 4, :], T1[0:SAMP, 0:HD], ACT.Copy).then_inc(v_rows_done, 1)
            act.activation(KNEW[:, :], T1[0:SAMP, HD:2 * HD], ACT.Copy).then_inc(v_rows_done, 1)
            for i in range(4):
                act.wait_ge(max_done, n(4, i + 1))
                s = SP_[:, POFF[i]:POFF[i] + (i + 1) * P]
                act.activation(s, s, ACT.Exp, bias=SM[:, 4 + i:5 + i], scale=1.0, accum_out=SM[:, 8 + i:9 + i]).then_inc(exp_done, 1)
            h = HEADS + hc if it is None else it * 2 + (HEADS + hc)
            for b in range(NB):
                act.wait_ge(k_turned, n(8, b + 1))
                act.activation(KTH[:, 0:NEAR], T0[:, 0:NEAR], ACT.Copy).then_inc(kh_done, 1)
                act.activation(KTH[:, NEAR:NEAR + 4 * FAR], T1[:, 0:4 * FAR], ACT.Copy).then_inc(kh_done, 1)
                if b == 0:
                    act.wait_ge(pv_done, n(1, 1))
                    act.activation(hb(h, 0, SEQ), BZ[:, 0:SEQ], ACT.Copy).then_inc(pv_read, 1)
                    hi(u + 2, it, 6)
            act.wait_ge(smax_done, n(1, 1))
            act.activation(SS[:, :], SS[:, :], ACT.Exp, bias=SM[0:SAMP, 15:16], scale=1.0, accum_out=SM[0:SAMP, 16:17]).then_inc(sexp_done, 1)
            hi(u + 3, it, 6)
            act.wait_ge(pvs_done, n(16, 16))
            act.activation(OT[:, :, :], BZ[:, 0:2 * P].rearrange("p (w d) -> p w d", w=2), ACT.Copy).then_inc(ot_done, 1)
        with act.Fori(0, HEADS // 2) as it:
            for hh in range(2):
                swa_head(hh, it)

        act.wait_ge(scratch_free, 1)
        act.wait_ge(gconst_in, 16 * 4)

        def gla_head(it, c, last):
            def n(per, d):
                return at(per * c + d, it, per)
            u = U_GLA + 3 + 6 * c
            g = GRP[:, 1]
            act.wait_ge(z_done, n(1, 1))
            bg = BG[:, c:c + 1] if it is None else BG[:, bass.ds(it, 1)]
            act.activation(LA[:, 0:SEQ], T0[:, 0:SEQ], ACT.Identity, bias=bg).then_inc(z_read, 1)
            act.activation(LA[:, SEQ:T], T1[:, 0:SAMP], ACT.Identity, bias=bg).then_inc(z_read, 1)
            act.wait_ge(z_read, n(2, 2))
            own.mark(act.activation(EA[:, :], LA[:, :], ACT.Abs))
            own.wait()
            own.mark(act.activation(EB[:, :], EA[:, :], ACT.Exp, scale=-1.0))
            own.wait()
            act.activation(EA[:, :], EB[:, :], ACT.Ln, bias=1.0).then_inc(e_done, 1)
            hi(u + 1, it, 6)
            act.wait_ge(la_done, n(1, 1))
            act.activation(EB[:, :], LA[:, :], ACT.Exp, scale=1.0 / TAU).then_inc(e_done, 1)
            act.activation(EA[:, :], LA[:, :], ACT.Exp, scale=-1.0 / TAU).then_inc(e_done, 1)
            own.mark(act.activation(ET[:, 0:NCH], LA[:, 0:SEQ].rearrange("p (c t) -> p c t", t=CH)[:, :, CH - 1], ACT.Exp, scale=1.0 / TAU))
            act.activation(ET[:, 8:16], samples(LA[:, SEQ:T])[:, :, NQ - 1], ACT.Exp, scale=1.0 / TAU).then_inc(e_done, 1)
            act.wait_ge(dt_done, n(2, 2))
            act.activation(EB[:, :], EB[:, :], ACT.Exp, scale=1.0 / TAU).then_inc(e_done, 1)

            def v_rows(w):
                act.wait_ge(gv_turned, n(2, w + 1))
                dv = slice(w * P, (w + 1) * P)
                act.activation(GVN[:, 0:4, dv], BO[:, :].rearrange("p (j d) -> p j d", j=4), ACT.Copy).then_inc(gv_done, 1)
                act.activation(GVN[0:SAMP, 4, dv], T1[0:SAMP, 0:P], ACT.Copy).then_inc(gv_done, 1)
            v_rows(0)
            hi(u + 2, it, 6)
            act.wait_ge(kn_turned, n(1, 1))
            act.activation(KN[:, 0:4, :], T0[:, :].rearrange("p (j d) -> p j d", j=4), ACT.Copy).then_inc(kn_done, 1)
            act.activation(KN[0:SAMP, 4, :], T1[0:SAMP, 0:P], ACT.Copy).then_inc(kn_done, 1)
            v_rows(1)
            hi(u + 3, it, 6)
            act.wait_ge(half_read, at(2 * u + 6, it, 12))
            for w in range(2):
                act.activation(g[:, 1 + w, :], g[:, 1 + w, :], ACT.Silu).then_inc(silu_done, 1)
            if not last:
                hi(u + 4, it, 6)
            act.wait_ge(o_done, n(1, 1))
            act.activation(EA[:, 0:SEQ], SA[:, 0:SEQ], ACT.Square).then_inc(sqg_done, 1)
            act.activation(EA[:, SEQ:T], T0[:, 0:SAMP], ACT.Square).then_inc(sqg_done, 1)
            act.activation(EB[:, 0:SEQ], SB[:, 0:SEQ], ACT.Square).then_inc(sqg_done, 1)
            act.activation(EB[:, SEQ:T], T0[:, SAMP:2 * SAMP], ACT.Square).then_inc(sqg_done, 1)
            if not last:
                hi(u + 5, it, 6)
            act.wait_ge(gms_done, n(2, 2))
            act.activation(EB[:, :], EB[:, :], ACT.Sqrt).then_inc(gsqrt_done, 1)
            if not last:
                hi(u + 6, it, 6)
        with act.Fori(0, GH - 1) as it:
            own.enter(it, 3)
            gla_head(it, 0, False)
            own.leave(GH - 1)
        gla_head(None, GH - 1, True)

        act.wait_ge(half_done, 2 * U_OUT)
        for i, k in enumerate([*range(8, KT), *range(8)]):
            if k < 8:
                act.wait_ge(mix_done, 2 * GH)
            act.activation(XH[:, k, :], hb(k), ACT.Copy).then_inc(mh_done, 1)

        def out_step(c, it=None, k=0):
            m = c - U_OUT
            hi(c + 1, it, k)
            act.wait_ge(half_read, at(2 * c + 2, it, 2 * k))
            if m:
                act.wait_ge(acc_done, at(m, it, k))
            act.activation(SQ[:, :], hb(m if it is None else it * k + m), ACT.Square).then_inc(hsq_done, 1)
        out_step(U_OUT)
        out_step(U_OUT + 1)
        with act.Fori(0, 7) as it:
            for i in range(2):
                out_step(U_OUT + 2 + i, it, 2)

        for k in range(KT):
            act.activation(XH[:, k, :], hb(k), ACT.Copy, scale=GF[:, k:k + 1]).then_inc(fh_done, 1)

        def used(c):
            if c < PAIR:
                return 2 * (c + 1)
            r, i = divmod(c - PAIR, PAIR + DOWN)
            return 16 + 48 * r + (2 * (i + 1) if i < PAIR else 16 + 8 * (i - PAIR + 1))

        def next_hi(c, it=None):
            i = c - U_FFN
            if i == 0:
                act.wait_ge(raw_ready[(c + 1) % 2], 16 * ((c + 1) // 2 + 1))
                act.wait_ge(half_done, 2 * U_FFN)
                act.activation(WH[(c + 1) % 2][:, :], RAW[(c + 1) % 2][:, :], ACT.Copy).then_inc(hi_done, 1)
            else:
                hi(c + 1, it, 24, ffn=used(i - 1))

        def up_post(g, gc, j, s, f, it=None):
            t = 2 * (GT * gc + j) + s
            act.wait_ge(fhalf_read, at(f + 2, it, 96))
            U, C = (UA, CA) if s == 0 else (UV, CV)
            tile = g * GT + (s * FT + j)
            w2 = WC[:, 2, tile:tile + 1] if it is None else WC[:, 2, bass.ds(tile, 1)]
            b = BC[:, tile:tile + 1] if it is None else BC[:, bass.ds(tile, 1)]
            if it is not None or gc * GT + j >= 1:
                act.wait_ge(prod_done, at(2 * (gc * GT + j), it, 16))
            act.activation(C[:, :], U[:, 2:UW], ACT.Identity, scale=w2, bias=b).then_inc(aff_done, 1)
            if s:
                act.wait_ge(conv_done, at(t, it, 16))
                act.activation(CA[:, :], CA[:, :], ACT.Silu).then_inc(silu2_done, 1)
                act.wait_ge(prod_done, at(2 * (gc * GT + j) + 2, it, 16))
                act.activation(AH[gc % 2][:, j, :], PR[:, :], ACT.Copy).then_inc(ah_done, 1)

        act.wait_ge(conv_in, 32)
        next_hi(U_FFN)
        act.wait_ge(ms_done, 4)
        act.activation(RN[:, :], RN[:, :], ACT.Sqrt).then_inc(sqrt_done, 1)
        for j in range(GT):
            for s in range(2):
                if j or s:
                    next_hi(U_FFN + 2 * j + s)
                up_post(0, 0, j, s, 2 * (2 * j + s))
        c0, f0 = U_FFN + PAIR, 2 * PAIR
        with act.Fori(0, (NG - 1) // 2) as it:
            for p in range(2):
                c, f = c0 + p * (PAIR + DOWN), f0 + p * 48
                for j in range(GT):
                    for s in range(2):
                        next_hi(c + 2 * j + s, it)
                        up_post(it * 2 + (1 + p), 1 + p, j, s, f + 2 * (2 * j + s), it)
                for i in range(DOWN):
                    next_hi(c + PAIR + i, it)
        c = U_FFN + NG * PAIR + (NG - 1) * DOWN
        for i in range(DOWN):
            if i < DOWN - 1:
                next_hi(c + i)
            for j in range(4):
                m = 4 * i + j
                act.wait_ge(fhalf_read, f0 + (NG - 1) * 48 + 2 * m + 2)
                act.wait_ge(acc_done, KT + m)
                act.activation(SQ[:, :], hb(m), ACT.Square).then_inc(hsq_done, 1)
        act.wait_ge(ms_done, 6)
        act.activation(RN[:, :], RN[:, :], ACT.Sqrt).then_inc(sqrt_done, 1)

    @block.vector
    def _(dve):
        own = Order(dve, dve_own)

        def lo(c, it=None, k=0):
            dve.wait_ge(hi_done, at(c + 1, it, k))
            dve.tensor_tensor(WL[c % 2][:, :], RAW[c % 2][:, :], WH[c % 2][:, :].bitcast(F32), ALU.subtract).then_inc(lo_done, 1)

        def mean_inv(rn_n):
            dve.wait_ge(sums_done, 2 * rn_n)
            for x in range(2):
                dve.tensor_scalar(RN[:, x * HALF:(x + 1) * HALF], PJ[x][:, 0:HALF], 1.0 / D, EPS, ALU.mult, ALU.add).then_inc(ms_done, 1)
            dve.wait_ge(sqrt_done, rn_n)
            dve.reciprocal(RN[:, :], RN[:, :]).then_inc(rn_done, 1)
            dve.wait_ge(rn_done, rn_n)

        def read_half(dst, x, scale, c, it=None, k=0):
            dve.wait_ge(half_done, at(2 * c + x + 1, it, 2 * k))
            t = slice(x * HALF, (x + 1) * HALF)
            dve.scalar_tensor_tensor(dst[:, t], PJ[x][:, 0:HALF], scale, RN[:, t], ALU.mult, ALU.mult).then_inc(half_read, 1)

        for k in range(KT):
            dve.wait_ge(xh_done, k + 1)
            dve.scalar_tensor_tensor(XL[:, k, :], hb(k), GA[:, k:k + 1], XH[:, k, :].bitcast(F32), ALU.mult, ALU.subtract).then_inc(xl_done, 1)
        dve.wait_ge(zs_done, 1)
        dve.tensor_tensor(ZL[:, :, :], ZRAW[:, :, :], ZH[:, :, :].bitcast(F32), ALU.subtract).then_inc(zs_done, 1)
        lo(0)
        lo(1)
        mean_inv(1)
        dve.wait_ge(za_half, 2)
        for x in range(2):
            t = slice(x * HALF, (x + 1) * HALF)
            dve.tensor_tensor(ZA[:, t], [SA, SB][x][0:RANK, 0:HALF], RN[0:RANK, t], ALU.mult).then_inc(za_done, 1)
        for u in range(3):
            read_half(GRP[:, 0, u], 0, SCALE if u == 0 else 1.0, u)
            read_half(GRP[:, 0, u], 1, SCALE if u == 0 else 1.0, u)
            if u < 2:
                lo(u + 2)

        def swa_head(hc, it):
            def n(per, c):
                return at(per * hc + c, it, 2 * per)
            u = 3 * hc + 3
            g = GRP[:, 1 - hc % 2]
            lo(u + 1, it, 6)
            dve.wait_ge(rows_free, n(1, 1))
            read_half(g[:, 0], 0, SCALE, u, it, 6)
            dve.wait_ge(tabp_in, n(16, 16))
            for i in range(4):
                w = (i + 1) * P
                s = SP_[:, POFF[i]:POFF[i] + w]
                dve.wait_ge(scores_done, n(4, i + 1))
                dve.sem_inc(passed, 1)
                own.mark(dve.tensor_tensor_reduce(s, [SA, SB, BO, BZ][i][:, 0:w], TABP[:, SEQ - w:SEQ], 1.0, NEG, ALU.add, ALU.max, SM[:, i:i + 1]))
                own.wait()
                dve.tensor_scalar(SM[:, 4 + i:5 + i], SM[:, i:i + 1], -1.0, None, ALU.mult).then_inc(max_done, 1)
            for i in range(4):
                s = SP_[:, POFF[i]:POFF[i] + (i + 1) * P]
                dve.wait_ge(exp_done, n(4, i + 1))
                own.mark(dve.reciprocal(SM[:, 18 + i:19 + i], SM[:, 8 + i:9 + i]))
                own.wait()
                dve.tensor_scalar(s, s, SM[:, 18 + i:19 + i], None, ALU.mult).then_inc(norm_done, 1)
            read_half(g[:, 0], 1, SCALE, u, it, 6)
            dve.wait_ge(probs_turned, n(1, 1))
            for i in range(4):
                src = [SA[:, 0:P], SA[:, P:3 * P], SB[:, 0:3 * P], BO[:, :]][i]
                dve.tensor_copy(PT[:, 0:i + 1, i * P:(i + 1) * P], src.rearrange("p (j t) -> p j t", t=P)).then_inc(pt_done, 1)
            for b in range(NB):
                for i, (bank_, cols) in enumerate(((T0, slice(0, NEAR)), (T1, slice(NEAR, NKEY - SAMP)))):
                    dve.wait_ge(kh_done, n(16, 2 * b + i + 1))
                    dve.tensor_tensor(KTL[:, cols], bank_[:, 0:cols.stop - cols.start], KTH[:, cols].bitcast(F32), ALU.subtract).then_inc(kl_done, 1)
                if b == 1:
                    lo(u + 2, it, 6)
                elif b == 2:
                    read_half(g[:, 1], 0, 1.0, u + 1, it, 6)
                elif b == 5:
                    read_half(g[:, 1], 1, 1.0, u + 1, it, 6)
            dve.wait_ge(qk_done, n(1, 1))
            dve.wait_ge(tabs_in, n(16, 16))
            own.mark(dve.tensor_tensor(SS[:, 0:NEAR], SA[SAMP:2 * SAMP, 0:NEAR], TABS[:, 0:NEAR], ALU.add))
            own.mark(dve.tensor_tensor(SS[:, NEAR:NKEY - SAMP], SB[SAMP:2 * SAMP, 0:4 * FAR], TABS[:, NEAR:NKEY - SAMP], ALU.add))
            own.mark(dve.tensor_copy(SS[:, NKEY - SAMP:NKEY], TABS[:, NKEY - SAMP:NKEY]))
            own.wait()
            dve.sem_inc(passed, 1)
            own.mark(dve.tensor_tensor_reduce(SS[:, 0:NEAR], SA[0:SAMP, 0:NEAR], SS[:, 0:NEAR], 1.0, NEG, ALU.add, ALU.max, SM[0:SAMP, 13:14]))
            own.mark(dve.tensor_tensor_reduce(SS[:, NEAR:NKEY], SB[0:SAMP, 0:NKEY - NEAR], SS[:, NEAR:NKEY], 1.0, NEG, ALU.add, ALU.max, SM[0:SAMP, 14:15]))
            own.wait()
            own.mark(dve.tensor_tensor(SM[0:SAMP, 13:14], SM[0:SAMP, 13:14], SM[0:SAMP, 14:15], ALU.max))
            own.wait()
            dve.tensor_scalar(SM[0:SAMP, 15:16], SM[0:SAMP, 13:14], -1.0, None, ALU.mult).then_inc(smax_done, 1)
            read_half(g[:, 2], 0, 1.0, u + 2, it, 6)
            dve.wait_ge(sexp_done, n(1, 1))
            own.mark(dve.reciprocal(SM[0:SAMP, 17:18], SM[0:SAMP, 16:17]))
            own.wait()
            dve.tensor_scalar(SS[:, :], SS[:, :], SM[0:SAMP, 17:18], None, ALU.mult).then_inc(snorm_done, 1)
            dve.wait_ge(sprobs_turned, n(1, 1))
            dve.tensor_copy(PTS[:, 0:4, :], T0[:, 0:4 * SAMP].rearrange("p (j t) -> p j t", j=4)).then_inc(pts_done, 1)
            dve.tensor_copy(PTS[0:FAR, 4:8, :], T0[0:FAR, 4 * SAMP:8 * SAMP].rearrange("p (j t) -> p j t", j=4)).then_inc(pts_done, 1)
            dve.tensor_copy(PTS[0:SAMP, 8, :], T0[0:SAMP, 8 * SAMP:9 * SAMP]).then_inc(pts_done, 1)
            lo(u + 3, it, 6)
            read_half(g[:, 2], 1, 1.0, u + 2, it, 6)
            h = HEADS + hc if it is None else it * 2 + (HEADS + hc)
            dve.wait_ge(ot_turned, n(1, 1))
            for w in range(2):
                first = (w + 1) * P + 16 * w
                old = BO[:, first:first + 4 * 36].rearrange("p (b x) -> p b x", x=36)[:, :, 0:NQ]
                own.mark(dve.tensor_copy(samples(hb(h, SEQ + 16 * w, 16)), old))
            own.wait()
            dve.tensor_tensor(hb(h, SEQ, SAMP), hb(h, SEQ, SAMP), BO[:, 0:SAMP], ALU.add).then_inc(pvs_read, 1)
        with dve.Fori(0, HEADS // 2) as it:
            own.enter(it, 34)
            for hh in range(2):
                swa_head(hh, it)
            own.leave(HEADS // 2)

        dve.wait_ge(scratch_free, 1)
        dve.wait_ge(gconst_in, 16 * 4)

        def gla_head(it, c, last):
            def n(per, d):
                return at(per * c + d, it, per)
            u = U_GLA + 3 + 6 * c
            g0, g1 = GRP[:, 0], GRP[:, 1]
            lo(u + 1, it, 6)
            dve.wait_ge(e_done, n(5, 1))
            own.mark(dve.scalar_tensor_tensor(LA[:, :], LA[:, :], 0.0, EA[:, :], ALU.min, ALU.subtract))
            own.wait()
            dve.tensor_tensor_scan(LA[:, :], RESET[:, :], LA[:, :], 0.0, ALU.mult, ALU.add).then_inc(la_done, 1)
            read_half(g1[:, 0], 0, 1.0, u, it, 6)
            dve.wait_ge(e_done, n(5, 2))
            dve.tensor_tensor(QD[:, :], g0[:, 0], EB[:, :], ALU.mult).then_inc(qd_done, 1)
            dve.wait_ge(e_done, n(5, 4))
            dve.wait_ge(qd_done, n(1, 1))

            def left(ap, width):
                v = ap.rearrange("p (c t) -> p c t", t=width)
                return v, v[:, :, width - 1:width]
            v, tot = left(LA[:, 0:SEQ], CH)
            dve.tensor_tensor(EB[:, 0:SEQ].rearrange("p (c t) -> p c t", t=CH), tot.broadcast_to([P, NCH, CH]), v, ALU.subtract).then_inc(dt_done, 1)
            v, tot = left(LA[:, SEQ:T], NQ)
            dve.tensor_tensor(samples(EB[:, SEQ:T]), tot.broadcast_to([P, NB, NQ]), v, ALU.subtract).then_inc(dt_done, 1)
            dve.tensor_tensor(KD[:, :], g0[:, 1], EA[:, :], ALU.mult).then_inc(kd_done, 1)
            read_half(g1[:, 0], 1, 1.0, u, it, 6)
            dve.wait_ge(e_done, n(5, 5))
            dve.wait_ge(kd_done, n(1, 1))
            dve.tensor_tensor(g0[:, 1], g0[:, 1], EB[:, :], ALU.mult).then_inc(ke_done, 1)
            dve.wait_ge(at_done, n(1, 1))
            dve.tensor_tensor(AT[:, 0:SEQ].rearrange("p (j t) -> p j t", t=P), SA[:, :].rearrange("p (j t) -> p j t", t=P),
                              PM[:, :].unsqueeze(1).broadcast_to([P, 4, P]), ALU.mult).then_inc(at_read, 1)
            dve.tensor_tensor(AT[0:SAMP, SEQ:T], SB[0:SAMP, 0:SAMP], SMK[:, :], ALU.mult).then_inc(at_read, 1)
            lo(u + 2, it, 6)
            read_half(g1[:, 1], 0, 1.0, u + 1, it, 6)

            def masked(i):
                for b in range(4):
                    ins = dve.tensor_scalar(VM[:, b, :], GVN[0:SAMP, 4, :], RM[:, 4 * i + b:4 * i + b + 1], None, ALU.mult)
                ins.then_inc(vm_done, 1)
            dve.wait_ge(gv_done, n(4, 4))
            masked(0)
            read_half(g1[:, 1], 1, 1.0, u + 1, it, 6)
            read_half(g1[:, 2], 0, 1.0, u + 2, it, 6)
            lo(u + 3, it, 6)
            dve.wait_ge(state_free, n(1, 1))
            dve.wait_ge(inc_done, n(1, 1))
            for ch in range(NCH):
                add = addition(ch)
                if ch == 0:
                    dve.tensor_copy(ST[:, 0, :], add).then_inc(state_done, 1)
                else:
                    dve.wait_ge(state_done, n(8, ch))
                    dve.scalar_tensor_tensor(ST[:, ch, :], ST[:, ch - 1, :], ET[:, ch:ch + 1], add, ALU.mult, ALU.add).then_inc(state_done, 1)
            read_half(g1[:, 2], 1, 1.0, u + 2, it, 6)
            if not last:
                read_half(g0[:, 0], 0, SCALE, u + 3, it, 6)
            dve.wait_ge(sqg_done, n(4, 4))
            dve.tensor_tensor(EA[:, :], EA[:, :], EB[:, :], ALU.add).then_inc(sq2_done, 1)
            if not last:
                lo(u + 4, it, 6)
                read_half(g0[:, 0], 1, SCALE, u + 3, it, 6)

            def sample_states(i):
                dve.wait_ge(us_done, n(2, i + 1))
                for b in range(4):
                    add = [T1, BO][b // 2][:, (b % 2) * DV:(b % 2 + 1) * DV]
                    s = S0[:, 4 * i + b, :]
                    ins = dve.scalar_tensor_tensor(s, s, ET[:, 8 + 4 * i + b:9 + 4 * i + b], add, ALU.mult, ALU.add)
                ins.then_inc(ss_done, 1)
            sample_states(0)
            dve.wait_ge(gsum_done, n(1, 1))
            dve.tensor_scalar(EB[:, 0:SEQ], BZ[:, 0:SEQ], 1.0 / DV, EPS, ALU.mult, ALU.add).then_inc(gms_done, 1)
            dve.tensor_scalar(EB[:, SEQ:T], T1[:, 0:SAMP], 1.0 / DV, EPS, ALU.mult, ALU.add).then_inc(gms_done, 1)
            masked(1)
            dve.wait_ge(gsqrt_done, n(1, 1))
            own.mark(dve.reciprocal(EB[:, :], EB[:, :]))
            own.wait()
            dve.wait_ge(silu_done, n(2, 2))
            for w in range(2):
                if w:
                    dve.wait_ge(mix_done, n(2, 1))
                gg = GG[:, 2 * c + w:2 * c + w + 1] if it is None else GG[:, bass.ds(it * 2 + w, 1)]
                own.mark(dve.scalar_tensor_tensor(EA[:, 0:SEQ], [SA, SB][w][:, 0:SEQ], gg, EB[:, 0:SEQ], ALU.mult, ALU.mult))
                own.mark(dve.scalar_tensor_tensor(EA[:, SEQ:T], T0[:, w * SAMP:(w + 1) * SAMP], gg, EB[:, SEQ:T], ALU.mult, ALU.mult))
                own.wait()
                tile = 2 * c + w if it is None else it * 2 + w
                dve.tensor_tensor(hb(tile), EA[:, :], g1[:, 1 + w, :], ALU.mult).then_inc(mix_done, 1)
            if not last:
                lo(u + 5, it, 6)
                read_half(g0[:, 1], 0, 1.0, u + 4, it, 6)
            sample_states(1)
            if not last:
                read_half(g0[:, 1], 1, 1.0, u + 4, it, 6)
                lo(u + 6, it, 6)
                read_half(g0[:, 2], 0, 1.0, u + 5, it, 6)
                read_half(g0[:, 2], 1, 1.0, u + 5, it, 6)
        with dve.Fori(0, GH - 1) as it:
            own.enter(it, 6)
            gla_head(it, 0, False)
            own.leave(GH - 1)
        gla_head(None, GH - 1, True)

        for i, k in enumerate([*range(8, KT), *range(8)]):
            dve.wait_ge(mh_done, i + 1)
            dve.tensor_tensor(XL[:, k, :], hb(k), XH[:, k, :].bitcast(F32), ALU.subtract).then_inc(ml_done, 1)

        def out_step(c, it=None, k=0):
            m = c - U_OUT
            lo(c + 1, it, k)
            for x in range(2):
                if x == 0:
                    dve.wait_ge(xr_in[m % 2], at(16 * (m // 2 + 1), it, 8 * k))
                    if m == 0:
                        dve.wait_ge(mh_done, KT)
                dve.wait_ge(half_done, at(2 * c + x + 1, it, 2 * k))
                dst = hb(m if it is None else it * k + m, x * HALF, HALF)
                t = slice(x * HALF, (x + 1) * HALF)
                dve.tensor_tensor(dst, PJ[x][:, 0:HALF], XR[m % 2][:, t], ALU.add).then_inc(half_read, 1)
        out_step(U_OUT)
        out_step(U_OUT + 1)
        with dve.Fori(0, 7) as it:
            for i in range(2):
                out_step(U_OUT + 2 + i, it, 2)
        for k in range(KT):
            dve.wait_ge(fh_done, k + 1)
            dve.scalar_tensor_tensor(XL[:, k, :], hb(k), GF[:, k:k + 1], XH[:, k, :].bitcast(F32), ALU.mult, ALU.subtract).then_inc(fl_done, 1)

        def up_post(gc, c, j, s, f, it=None, g=None):
            t = 2 * (GT * gc + j) + s
            U, C = (UA, CA) if s == 0 else (UV, CV)
            b0, b1 = bank[f % 8], bank[(f + 1) % 8]
            if it is not None or t >= 2:
                dve.wait_ge(co_ready, at(t - 1, it, 16))
            if j == 0 and s == 0:
                dve.wait_ge(ci_in[gc % 2], at(16 * (gc // 2 + 1), it, 16))
            dve.tensor_copy(U[:, 2 + SEQ:UW].rearrange("p (b x) -> p b x", x=6)[:, :, 0:2],
                            CI[gc % 2][:, s, j, :].rearrange("p (b x) -> p b x", x=2))
            dve.wait_ge(fhalf_done, at(f + 1, it, 96))
            dve.tensor_tensor(U[:, 2:2 + HALF], b0[:, 0:HALF], RN[:, 0:HALF], ALU.mult).then_inc(fhalf_read, 1)
            dve.wait_ge(fhalf_done, at(f + 2, it, 96))
            dve.tensor_tensor(U[:, 2 + HALF:2 + SEQ], b1[:, 0:SEQ - HALF], RN[:, HALF:SEQ], ALU.mult)
            dve.tensor_tensor(U[:, 2 + SEQ:UW].rearrange("p (b x) -> p b x", x=6)[:, :, 2:6], samples(b1[:, SEQ - HALF:HALF]),
                              samples(RN[:, SEQ:T]), ALU.mult).then_inc(fhalf_read, 1)
            dve.wait_ge(aff_done, at(t + 1, it, 16))
            tile = s * FT + j if it is None else g * GT + (s * FT + j)
            w = [WC[:, i, tile:tile + 1] if it is None else WC[:, i, bass.ds(tile, 1)] for i in range(2)]
            own.mark(dve.scalar_tensor_tensor(C[:, :], U[:, 1:UW - 1], w[1], C[:, :], ALU.mult, ALU.add))
            own.wait()
            dve.scalar_tensor_tensor(C[:, :], U[:, 0:UW - 2], w[0], C[:, :], ALU.mult, ALU.add).then_inc(conv_done, 1)
            if s:
                dve.wait_ge(conv_done, at(t + 1, it, 16))
                dve.wait_ge(silu2_done, at(GT * gc + j + 1, it, 8))
                dve.tensor_tensor(PR[:, 0:SEQ], CA[:, 0:SEQ], CV[:, 0:SEQ], ALU.mult).then_inc(prod_done, 1)
                ca, cv = (C_[:, SEQ:CW].rearrange("p (b x) -> p b x", x=6)[:, :, 2:6] for C_ in (CA, CV))
                dve.tensor_tensor(samples(PR[:, SEQ:T]), ca, cv, ALU.mult).then_inc(prod_done, 1)
                dve.wait_ge(prod_done, at(2 * (GT * gc + j) + 2, it, 16))
                dve.wait_ge(ah_done, at(GT * gc + j + 1, it, 8))
                dve.tensor_tensor(AL[gc % 2][:, j, :], PR[:, :], AH[gc % 2][:, j, :].bitcast(F32), ALU.subtract).then_inc(al_done, 1)

        for U in (UA, UV):
            own.mark(dve.memset(U[:, 0:2], 0.0))
        lo(U_FFN + 1)
        mean_inv(2)
        for j in range(GT):
            for s in range(2):
                if j or s:
                    lo(U_FFN + 2 * j + s + 1)
                up_post(0, U_FFN, j, s, 2 * (2 * j + s))
        c0, f0 = U_FFN + PAIR, 2 * PAIR

        def down_post(c, f, m4, nxt, it=None):
            if nxt:
                lo(c + 1, it, 24)
            for j in range(4):
                for x in range(2):
                    n = f + 2 * j + x
                    dve.wait_ge(fhalf_done, at(n + 1, it, 96))
                    d = hb(4 * m4 + j, x * HALF, HALF)
                    dve.tensor_tensor(d, d, bank[n % 8][:, 0:HALF], ALU.add).then_inc(fhalf_read, 1)
        with dve.Fori(0, (NG - 1) // 2) as it:
            own.enter(it, 2 * PAIR)
            for p in range(2):
                c, f = c0 + p * (PAIR + DOWN), f0 + p * 48
                for j in range(GT):
                    for s in range(2):
                        i = 2 * j + s
                        lo(c + i + 1, it, 24)
                        up_post(1 + p, c, j, s, f + 2 * i, it, it * 2 + (1 + p))
                for i in range(DOWN):
                    down_post(c + PAIR + i, f + 16 + 8 * i, i, True, it)
            own.leave((NG - 1) // 2)
        c, f = U_FFN + NG * PAIR + (NG - 1) * DOWN, f0 + (NG - 1) * 48
        for i in range(DOWN):
            down_post(c + i, f + 8 * i, i, i < DOWN - 1)
        mean_inv(3)
        for k in range(KT):
            dve.scalar_tensor_tensor(hb(k), hb(k), GZ[:, k:k + 1], RN[:, :], ALU.mult, ALU.mult).then_inc(y_done, 1)

    @block.gpsimd
    def _(pool):
        def alone():
            pool.sem_inc(passed, 1)
        pool.memset(QP[:, :].bitcast(F32), 0.0).then_inc(qp_zero, 1)
        pool.wait_ge(qp_zero, 1)
        pool.dma_start(TABP[:, :], A["tab_prompt"][0]).then_inc(tabp_in, 16)
        pool.dma_start(TABS[:, :], A["tab_sample"][0]).then_inc(tabs_in, 16)

        pool.sem_inc(rows_free, 1)
        pool.sem_inc(state_free, 1)

        def swa_head(hc, it):
            def n(per, c):
                return at(per * hc + c, it, 2 * per)
            g = GRP[:, hc % 2]
            h = hc if it is None else it * 2 + hc
            pool.wait_ge(half_read, n(6, 2))
            alone()
            qp = QP[:, :].rearrange("p (b x) -> p b x", x=2 * SAMP + NQ)
            pool.tensor_copy(qp[:, :, 0:NQ], samples(g[:, 0, SEQ:T])).then_inc(qp_high, 1)
            pool.wait_ge(qp_high, n(1, 1))
            pool.tensor_tensor(qp[:, :, SAMP:SAMP + NQ], samples(g[:, 0, SEQ:T]), qp[:, :, 0:NQ].bitcast(F32), ALU.subtract).then_inc(qp_done, 1)
            pool.wait_ge(v_rows_done, n(3, 3))
            alone()

            def rows(name):
                v = O[name][:, PAST - NQ:PAST]
                return v[:, :, bass.ds(h, 1), :].rearrange("b i h d -> b i (h d)")
            pool.dma_start(rows("k_sample"), KNEW[:, :]).then_inc(head_stored, 16)
            pool.dma_start(rows("v_sample"), VN[0:SAMP, 4, :]).then_inc(head_stored, 16)
            pool.dma_start(O["v_prompt"].rearrange("(j p) h d -> p j h d", p=P)[:, :, bass.ds(h, 1), :].rearrange("p j h d -> p j (h d)"),
                           VN[:, 0:4, :]).then_inc(head_stored, 16)
            pool.dma_start(O["k_prompt_t"][bass.ds(h, 1)].rearrange("h p t -> (h p) t"), g[:, 1, 0:SEQ]).then_inc(head_stored, 16)
            pool.wait_ge(max_done, n(4, 4))
            alone()
            pool.dma_start(TABP[:, :], A["tab_prompt"][bass.ds(h + 1, 1)].rearrange("h p t -> (h p) t")).then_inc(tabp_in, 16)
            pool.wait_ge(smax_done, n(1, 1))
            alone()
            pool.dma_start(TABS[:, :], A["tab_sample"][bass.ds(h + 1, 1)].rearrange("h p t -> (h p) t")).then_inc(tabs_in, 16)
            pool.wait_ge(head_stored, n(64, 64))
            pool.sem_inc(rows_free, 1)
        with pool.Fori(0, HEADS // 2) as it:
            for hh in range(2):
                swa_head(hh, it)

        pool.wait_ge(head_stored, 64 * HEADS)
        pool.wait_ge(tabp_in, 16 * (HEADS + 1))
        pool.wait_ge(tabs_in, 16 * (HEADS + 1))
        pool.wait_ge(pvs_read, HEADS)
        pool.dma_start(RESET[:, :], A["reset"]).then_inc(gconst_in, 16)
        pool.dma_start(PM[:, :], A["pair_mask"]).then_inc(gconst_in, 16)
        pool.dma_start(SMK[:, :], A["sample_mask"]).then_inc(gconst_in, 16)
        pool.dma_start(RM[:, :], A["row_mask"]).then_inc(gconst_in, 16)
        pool.sem_inc(scratch_free, 1)

        def gla_head(it, c):
            def n(per, d):
                return at(per * c + d, it, per)
            h = c if it is None else it
            pool.dma_start(WG[:, :], A["w_gate"][:, bass.ds(h * DK, DK)] if it is not None else A["w_gate"][:, h * DK:(h + 1) * DK]).then_inc(wg_in, 16)
            src = A["state_gla"][:, bass.ds(h, 1)] if it is not None else A["state_gla"][:, h:h + 1]
            pool.dma_start(S0[:, :, :], src.rearrange("b h p v -> (h p) b v")).then_inc(s0_in, 16)
            pool.wait_ge(state_done, n(8, 8))
            alone()
            dst = O["state_prompt"][bass.ds(h, 1)] if it is not None else O["state_prompt"][h:h + 1]
            pool.dma_start(dst.rearrange("h p v -> (h p) v"), ST[:, NCH - 1, :]).then_inc(state_stored, 16)
            pool.wait_ge(ss_done, n(2, 2))
            alone()
            dst = O["state_sample"][:, bass.ds(h, 1)] if it is not None else O["state_sample"][:, h:h + 1]
            pool.dma_start(dst.rearrange("b h p v -> (h p) b v"), S0[:, :, :]).then_inc(sstate_stored, 16)
            pool.wait_ge(state_stored, n(16, 16))
            pool.wait_ge(sstate_stored, n(16, 16))
            pool.sem_inc(state_free, 1)
        with pool.Fori(0, GH - 1) as it:
            gla_head(it, 0)
        gla_head(None, GH - 1)

        def add_squares(c, it=None, k=0, first=False):
            pool.wait_ge(hsq_done, at(c + 1, it, k))
            alone()
            if first:
                if c:
                    pool.wait_ge(sums_done, 4)
                pool.tensor_copy(ACC[:, :], SQ[:, :]).then_inc(acc_done, 1)
            else:
                pool.wait_ge(acc_done, at(c, it, k))
                alone()
                pool.tensor_tensor(ACC[:, :], ACC[:, :], SQ[:, :], ALU.add).then_inc(acc_done, 1)
        pool.wait_ge(mix_done, 2 * GH)
        add_squares(0, first=True)
        with pool.Fori(0, KT - 1) as it:
            add_squares(1, it, 1)

        cout = O["conv_out"].rearrange("p (s n) x -> p s n x", s=2)

        def keep_rows(g, gc, f, it=None):
            if gc:
                pool.wait_ge(co_stored, at(16 * gc, it, 32))
                alone()
            for j in range(GT):
                for s in range(2):
                    t = 2 * (GT * gc + j) + s
                    U = UA if s == 0 else UV
                    pool.wait_ge(fhalf_read, at(f + 2 * (2 * j + s) + 2, it, 96))
                    alone()
                    own.mark(pool.tensor_copy(CO[gc % 2][:, s, j, 0:2], U[:, SEQ:SEQ + 2]))
                    pool.tensor_copy(CO[gc % 2][:, s, j, 2:18].rearrange("p (b x) -> p b x", x=2),
                                     U[:, 2 + SEQ:UW].rearrange("p (b x) -> p b x", x=6)[:, :, 4:6]).then_inc(co_ready, 1)
            pool.wait_ge(co_ready, at(PAIR * (gc + 1), it, 16))
            own.wait()
            alone()
            dst = cout[:, :, bass.ds(g * GT, GT), :] if it is not None else cout[:, :, g * GT:(g + 1) * GT, :]
            pool.dma_start(dst, CO[gc % 2][:, :, :, :]).then_inc(co_stored, 16)
        own = Order(pool, pool_own)
        keep_rows(0, 0, 0)
        with pool.Fori(0, (NG - 1) // 2) as it:
            own.enter(it, 16)
            for p in range(2):
                keep_rows(it * 2 + (1 + p), 1 + p, 2 * PAIR + 48 * p, it)
            own.leave((NG - 1) // 2)
        for m in range(KT):
            add_squares(KT + m, first=m == 0)
        pool.wait_ge(co_stored, 16 * NG)
        pool.wait_ge(head_stored, 64 * HEADS)
        pool.wait_ge(state_stored, 16 * GH)
        pool.wait_ge(sstate_stored, 16 * GH)

    block.__exit__(None, None, None)


def _multiplicity(d):
    return sum(((d >= 0) & (d <= w) & (d % s == 0)).astype(np.int64) for w, s in ((128, 1), (512, 4), (2048, 16)))


def _bias(d, ok=True):
    c = np.where(ok, _multiplicity(d), 0)
    out = []
    for h in range(HEADS):
        slope = 2.0 ** (-8.0 * (h + 1) / HEADS)
        out.append(np.where(c > 0, -slope * d + np.log(np.maximum(c, 1)), NEG))
    out.append(out[-1])
    return np.stack(out).astype(np.float32)


def _constants():
    p = np.arange(P)
    tab_prompt = _bias(p[:, None] + (SEQ - P) - np.arange(SEQ)[None, :])
    pos = np.concatenate([
        (PAST - NEAR + 4 * np.arange(P)[None, :] + np.arange(4)[:, None]).ravel(),
        (16 * np.arange(FAR)[None, :] + np.arange(4)[:, None]).ravel(),
        PAST + np.arange(SAMP) % NQ])
    owner = np.concatenate([np.full(NKEY - SAMP, -1), np.arange(SAMP) // NQ])
    r = np.arange(SAMP)
    ok = (owner[None, :] < 0) | (owner[None, :] == r[:, None] // NQ)
    tab_sample = _bias(PAST + (r % NQ)[:, None] - pos[None, :], ok)
    t = np.arange(T)
    start = np.where(t < SEQ, t % CH == 0, (t - SEQ) % NQ == 0)
    return {
        "tab_prompt": tab_prompt,
        "tab_sample": tab_sample,
        "reset": np.repeat(np.where(start, 0.0, 1.0)[None, :], P, 0).astype(np.float32),
        "pair_mask": ((p[:, None] // CH == p[None, :] // CH) & (p[:, None] <= p[None, :])).astype(np.float32),
        "sample_mask": ((r[:, None] // NQ == r[None, :] // NQ) & (r[:, None] <= r[None, :])).astype(np.float32),
        "row_mask": (r[:, None] // NQ == np.arange(NB)[None, :]).astype(np.float32),
        "ident": np.eye(P, dtype=np.float32),
        "ones": np.ones((P, P), np.float32),
    }


_OUTS = {
    "y_t": (P, KT, T), "state_prompt": (GH, DK, DV), "state_sample": (NB, GH, DK, DV),
    "k_prompt_t": (HEADS, HD, SEQ), "k_sample": (NB, PAST, HEADS, HD), "v_prompt": (SEQ, HEADS, HD),
    "v_sample": (NB, PAST, HEADS, HD), "conv_out": (P, 2 * FT, 18),
}


def kernel(**inputs):
    import concourse.bacc as _bacc
    from concourse.bass_utils import run_bass_kernel_spmd as _run

    def tiles(v):
        v = np.asarray(v)
        return v.reshape(*v.shape[:-1], -1, P)

    x = np.concatenate([np.asarray(inputs["x_prompt"])[0], np.asarray(inputs["x_sample"]).reshape(SAMP, D)])
    conv = np.asarray(inputs["state_ffn_conv"])[0].reshape(NB * 2, 2 * FT, P)
    arrays = {
        "x_t": x.reshape(T, KT, P).transpose(2, 1, 0),
        "state_gla": np.asarray(inputs["state_gla"])[0],
        "cache_swa_k": np.asarray(inputs["cache_swa_k"])[0],
        "cache_swa_v": np.asarray(inputs["cache_swa_v"])[0],
        "conv_in": conv.transpose(2, 1, 0),
        "g_attn": tiles(inputs["g_attn_norm"])[0].T, "g_ffn": tiles(inputs["g_ffn_norm"])[0].T,
        "g_final": tiles(inputs["g_final"]).T, "g_gla": tiles(inputs["g_gla_norm"])[0].T,
        "b_gate": tiles(inputs["b_gate"])[0].T,
        "w_in": np.asarray(inputs["w_in"])[0], "w_gate": np.asarray(inputs["w_gate_up"])[0],
        "w_out": np.asarray(inputs["w_out"])[0], "w_up": np.asarray(inputs["w_up"])[0],
        "w_down": np.asarray(inputs["w_down"])[0],
        "w_conv": tiles(inputs["w_conv"])[0].transpose(2, 0, 1),
        "b_conv": tiles(inputs["b_conv"])[0].T,
        **_constants(),
    }
    arrays = {k: np.ascontiguousarray(v) for k, v in arrays.items()}
    nc = _bacc.Bacc("TRN2", target_bir_lowering=False, num_devices=1)
    A = {k: nc.dram_tensor(f"in_{k}", v.shape, mybir.dt.from_np(v.dtype), kind="ExternalInput").ap() for k, v in arrays.items()}
    O = {k: nc.dram_tensor(f"out_{k}", s, F32, kind="ExternalOutput").ap() for k, s in _OUTS.items()}
    build(nc, A, O)
    r = _run(nc, [{f"in_{k}": v for k, v in arrays.items()}], core_ids=[0]).results[0]
    got = {k: np.asarray(r[f"out_{k}"]) for k in _OUTS}
    y = got["y_t"].transpose(2, 1, 0).reshape(T, D)
    rows = got["conv_out"].transpose(2, 1, 0).reshape(18, 2 * DFF)
    return (y[:SEQ][None], y[SEQ:].reshape(NB, NQ, D),
            got["state_prompt"][None, None], got["state_sample"][None],
            got["k_prompt_t"].transpose(2, 0, 1)[None, None], got["k_sample"][None],
            got["v_prompt"][None, None], got["v_sample"][None],
            rows[:2][None, None], rows[2:].reshape(NB, 2, 2 * DFF)[None])
```

```python
import concourse.bass as bass
import numpy as np
from concourse import mybir

F32 = mybir.dt.float32
F32R = mybir.dt.float32r
ACT = mybir.ActivationFunctionType
ALU = mybir.AluOpType

P = 128
D = 2048
KT = D // P
SEQ, NB, NQ = 512, 8, 4
SAMP = NB * NQ
T = SEQ + SAMP
HALF = T // 2
HEADS, HD = 8, 128
GH, DK, DV = 4, 128, 256
CH = 64
NCH = SEQ // CH
RANK = 16
TAU = 16.0
DFF = 5632
FT = DFF // P
GT = 4
NG = FT // GT
PAST = 2048
EPS = 1e-6
SCALE = float(HD) ** -0.5
UNIT = 2048

C_QA, C_KA, C_VA, C_GA, C_ZA = 0, 512, 1024, 2048, 3072
C_QB = C_ZA + RANK
C_KB, C_VB = C_QB + 1024, C_QB + 2048
IN_COLS = C_VB + 1024

U_GLA = 3 * HEADS
U_OUT = U_GLA + 6 * GH
U_FFN = U_OUT + KT
PAIR = 2 * GT
DOWN = 4

NEAR = 512
FAR = (PAST - NEAR) // 16
NKEY = NEAR + 4 * FAR + SAMP
NEG = -1.0e30

CHUNK_ROWS = 146
COPIES = (PAST - NQ) // CHUNK_ROWS


def at(c, it=None, k=0):
    return c if it is None else it * k + c


class Order:

    def __init__(self, eng, sem):
        self.eng, self.sem, self.base, self.n = eng, sem, 0, 0

    def mark(self, ins):
        ins.then_inc(self.sem, 1)
        self.n += 1

    def wait(self):
        self.eng.wait_ge(self.sem, self.base + self.n)

    def enter(self, it, per):
        self.start = self.base + self.n
        self.base, self.n, self.per = it * per + self.start, 0, per

    def leave(self, times):
        assert self.n == self.per, (self.n, self.per)
        self.base, self.n = self.start + times * self.per, 0


def build(nc, A, O):
    base = (nc.sbuf_base + 31) // 32 * 32
    end = 229344

    def place(name, shape, dt, off):
        n = int(np.prod(shape[1:])) * 4
        assert base + off + n <= end, (name, base + off + n - end)
        return nc.alloc_sbuf_tensor_at(name, shape, dt, offset=base + off), off + (n + 31) // 32 * 32

    o = 0
    XH, o = place("x_high", [P, KT, T], F32R, o)
    XL, o = place("x_low", [P, KT, T], F32R, o)
    o_hb = o
    HB, o = place("residual", [P, KT * T], F32, o)
    RAW, WH, WL = [None, None], [None, None], [None, None]
    for s in range(2):
        RAW[s], o = place(f"w_raw{s}", [P, UNIT], F32, o)
        WH[s], o = place(f"w_high{s}", [P, UNIT], F32R, o)
        WL[s], o = place(f"w_low{s}", [P, UNIT], F32R, o)
    o_za = o
    ZA, o = place("gate_rank", [RANK, T], F32, o)
    ACC, _ = place("square_sum", [P, T], F32, o_za)
    RN, o = place("inv_rms", [P, T], F32, o)
    IDENT, o = place("ident", [P, P], F32, o)
    ONES, o = place("ones", [P, P], F32, o)
    GA, o = place("g_attn", [P, KT], F32, o)
    GF, o = place("g_ffn", [P, KT], F32, o)
    GZ, o = place("g_final", [P, KT], F32, o)
    GG, o = place("g_gla", [P, 2 * GH], F32, o)
    BG, o = place("b_gate", [P, GH], F32, o)
    SM, o = place("stats", [P, 24], F32, o)
    o_scr = o

    GRP, o = place("proj", [P, 2, 3, T], F32, o_scr)
    o_att = o
    VN, o = place("v_rows", [P, 5, HD], F32, o)
    KNEW, o = place("k_new_rows", [SAMP, HD], F32, o)
    SP_, o = place("probs", [P, 1280], F32, o)
    o_pt = o
    PT, o = place("probs_t", [P, 4, SEQ], F32, o)
    TABP, o = place("bias_prompt", [P, SEQ], F32, o)
    TABS, o = place("bias_sample", [SAMP, NKEY], F32, o)
    o_kt = o
    KTH, o = place("k_t_high", [P, NKEY - SAMP], F32R, o)
    KTL, o = place("k_t_low", [P, NKEY - SAMP], F32R, o)
    SS, o = place("probs_sample", [SAMP, NKEY], F32, o)
    PTS, o = place("probs_sample_t", [P, 9, SAMP], F32, o)
    QP, o = place("q_padded", [P, NB * (2 * SAMP + NQ)], F32R, o)
    OT, o = place("mixed_rows", [P, 2, P], F32, o)
    o_reset = o
    RESET, o = place("chunk_starts", [P, T], F32, o)
    PM, o = place("causal_pair", [P, P], F32, o)
    SMK, o = place("causal_sample", [SAMP, SAMP], F32, o)
    RM, o = place("row_of_sample", [SAMP, NB], F32, o)
    KR, VR = [None, None], [None] * 4
    VR[2], r = place("v_cache_rows2", [P, 8, HD], F32, o_pt)
    VR[3], r = place("v_cache_rows3", [P, 8, HD], F32, r)
    assert r - o_pt <= 4 * SEQ * 4
    r = o_hb
    for s in range(2):
        KR[s], r = place(f"k_rows{s}", [P, 8, HD], F32, r)
        VR[s], r = place(f"v_cache_rows{s}", [P, 8, HD], F32, r)
    WG, r = place("w_gate", [RANK, DK], F32, r)
    assert r - o_hb <= 8 * T * 4
    o = o_kt
    ZRAW, o = place("za_raw", [P, KT, RANK], F32, o)
    ZZ, o = place("za_parts", [P, KT, 2 * SAMP], F32R, o)

    o = o_att
    QD, o = place("q_decayed", [P, T], F32, o)
    KD, o = place("k_decayed", [P, T], F32, o)
    EA, o = place("tmp_a", [P, T], F32, o)
    EB, o = place("tmp_b", [P, T], F32, o)
    o_la = o
    KN, o = place("k_to_end_rows", [P, 5, DK], F32, o)
    LA, _ = place("log_decay", [P, T], F32, o_la)
    GVN, o = place("gla_v_rows", [P, 5, DV], F32, o)
    ST, o = place("states", [P, NCH, DV], F32, o)
    S0, o = place("states_sample", [P, NB, DV], F32, o)
    ET, o = place("decay_total", [P, 16], F32, o)
    VM, o = place("v_masked", [SAMP, 4, DV], F32, o)
    OS, o = place("outputs_sample", [P, 2, SAMP], F32, o)
    assert o <= o_reset
    AT = KD
    OR = KD

    o = o_scr
    AH, AL = [None, None], [None, None]
    for s in range(2):
        AH[s], o = place(f"act_high{s}", [P, GT, T], F32R, o)
        AL[s], o = place(f"act_low{s}", [P, GT, T], F32R, o)
    UW = 2 + SEQ + NB * 6
    CW = UW - 2
    UA, o = place("u_gate", [P, UW], F32, o)
    UV, o = place("u_value", [P, UW], F32, o)
    CA, o = place("conv_gate", [P, CW], F32, o)
    CV, o = place("conv_value", [P, CW], F32, o)
    XR = [None, None]
    XR[0], _ = place("x_again0", [P, T], F32, o_reset)
    XR[1], _ = place("x_again1", [P, T], F32, o_la)
    SQ, o = place("squares", [P, T], F32, o)
    PR = SQ
    WC, o = place("w_conv", [P, 3, 2 * FT], F32, o)
    BC, o = place("b_conv", [P, 2 * FT], F32, o)
    CI = [None, None]
    CI[0], o = place("conv_in0", [P, 2, GT, 16], F32, o)
    CI[1], o = place("conv_in1", [P, 2, GT, 16], F32, o)
    CO = [None, None]
    CO[0], o = place("conv_out0", [P, 2, GT, 18], F32, o)
    CO[1], o = place("conv_out1", [P, 2, GT, 18], F32, o)
    assert o <= o_reset

    bank = [nc.alloc_psum_tensor(n, [P, 512], F32) for n in ("bSA", "bSB", "bO", "bZ", "bT0", "bT1", "bPA", "bPB")]
    SA, SB, BO, BZ, T0, T1, PA, PB = bank
    PJ = [PA, PB]

    def sem(name):
        return nc.alloc_semaphore(name)

    raw_ready = [sem("raw_ready0"), sem("raw_ready1")]
    x_in, ga_in, consts_in, za_in = [sem(f"x_in{i}") for i in range(4)], sem("ga_in"), sem("consts_in"), sem("za_in")
    hi_done, lo_done = sem("hi_done"), sem("lo_done")
    xh_done, xl_done, sq_done = sem("xh_done"), sem("xl_done"), sem("sq_done")
    zs_done = sem("zs_done")
    sums_done, ms_done, sqrt_done, rn_done = sem("sums_done"), sem("ms_done"), sem("sqrt_done"), sem("rn_done")
    za_half, za_done = sem("za_half"), sem("za_done")
    half_done, half_read = sem("half_done"), sem("half_read")
    v_turned, v_rows_done = sem("v_turned"), sem("v_rows_done")
    scores_done, max_done, exp_done, norm_done = sem("scores_done"), sem("max_done"), sem("exp_done"), sem("norm_done")
    probs_turned, pt_done = sem("probs_turned"), sem("pt_done")
    k_in, vnear_in, vfar_in = [sem("k_in0"), sem("k_in1")], [sem(f"vnear_in{i}") for i in range(4)], [sem(f"vfar_in{i}") for i in range(4)]
    rows_free, state_free = sem("rows_free"), sem("state_free")
    k_turned, kh_done, kl_done = sem("k_turned"), sem("kh_done"), sem("kl_done")
    qk_done, qp_done, qp_high = sem("qk_done"), sem("qp_done"), sem("qp_high")
    smax_done, sexp_done, snorm_done = sem("smax_done"), sem("sexp_done"), sem("snorm_done")
    sprobs_turned, pts_done = sem("sprobs_turned"), sem("pts_done")
    pv_done, pv_read, pvs_done, pvs_read = sem("pv_done"), sem("pv_read"), sem("pvs_done"), sem("pvs_read")
    ot_done, ot_turned = sem("ot_done"), sem("ot_turned")
    tabp_in, tabs_in, head_stored = sem("tabp_in"), sem("tabs_in"), sem("head_stored")
    qp_zero = sem("qp_zero")
    scratch_free, gconst_in, wg_in, s0_in = sem("scratch_free"), sem("gconst_in"), sem("wg_in"), sem("s0_in")
    z_done, z_read, e_done = sem("z_done"), sem("z_read"), sem("e_done")
    qd_done, kd_done, ke_done, dt_done, la_done = sem("qd_done"), sem("kd_done"), sem("ke_done"), sem("dt_done"), sem("la_done")
    gv_turned, gv_done = sem("gv_turned"), sem("gv_done")
    at_done, at_read, kn_turned, kn_done = sem("at_done"), sem("at_read"), sem("kn_turned"), sem("kn_done")
    inc_done, state_done, o_done, sqg_done = sem("inc_done"), sem("state_done"), sem("o_done"), sem("sqg_done")
    or_done, or_turned, os_done = sem("or_done"), sem("or_turned"), sem("os_done")
    vm_done, us_done, ss_done = sem("vm_done"), sem("us_done"), sem("ss_done")
    sq2_done, gsum_done, gms_done, gsqrt_done = sem("sq2_done"), sem("gsum_done"), sem("gms_done"), sem("gsqrt_done")
    silu_done, mix_done, state_stored, sstate_stored = sem("silu_done"), sem("mix_done"), sem("state_stored"), sem("sstate_stored")
    mh_done, ml_done, xr_in = sem("mh_done"), sem("ml_done"), [sem("xr_in0"), sem("xr_in1")]
    hsq_done, acc_done = sem("hsq_done"), sem("acc_done")
    fh_done, fl_done = sem("fh_done"), sem("fl_done")
    fhalf_done, fhalf_read = sem("fhalf_done"), sem("fhalf_read")
    ci_in, co_ready, co_stored, conv_in = [sem("ci_in0"), sem("ci_in1")], sem("co_ready"), sem("co_stored"), sem("conv_in")
    aff_done, conv_done, silu2_done, prod_done = sem("aff_done"), sem("conv_done"), sem("silu2_done"), sem("prod_done")
    ah_done, al_done = sem("ah_done"), sem("al_done")
    y_done, out_stored, copied = sem("y_done"), sem("out_stored"), sem("copied")
    passed = sem("passed")
    act_own, dve_own, pool_own = sem("act_own"), sem("dve_own"), sem("pool_own")

    def w_cols(w, col):
        return w.rearrange("(k p) n -> p k n", p=P)[:, :, bass.ds(col, P) if not isinstance(col, int) else slice(col, col + P)]

    def raw3(s):
        return RAW[s][:, :].rearrange("p (k n) -> p k n", k=KT)

    def raw4(s):
        return RAW[s][:, :].rearrange("p (k n) -> p k n", k=GT)

    def hb(tile, lo=0, n=T):
        start = tile * T + lo
        return HB[:, start:start + n] if isinstance(tile, int) else HB[:, bass.ds(start, n)]

    def samples(ap):
        return ap.rearrange("p (b i) -> p b i", i=NQ)

    def addition(ch):
        j = (ch // 2) % 2
        return [T0, T1, BO, BZ][2 * (ch % 2) + ch // 4][:, j * DV:(j + 1) * DV]

    SQUARED = (0, 0, 2, 5, 7)
    MIX_ORDER, READY = [*range(8, KT), *range(8)], KT - 2
    POFF = [0, 128, 384, 768]
    block = nc.Block()
    block.__enter__()

    @block.sync
    def _(sp):
        def load_unit(src, dst, c, it=None, k=0):
            if c >= 2:
                sp.wait_ge(lo_done, at(c - 1, it, k))
            sp.dma_start(dst(c % 2), src).then_inc(raw_ready[c % 2], 16)

        def copy_cache(kv, b, j):
            name = "cache_swa_k" if kv == 0 else "cache_swa_v"
            oname = "k_sample" if kv == 0 else "v_sample"
            n = CHUNK_ROWS * HEADS * HD
            row = HEADS * HD

            def flat(ap, first):
                v = ap.rearrange("b r h d -> b (r h d)")
                v = v[b:b + 1] if isinstance(b, int) else v[bass.ds(b, 1)]
                lo = first * row
                return v[:, lo:lo + n].rearrange("b (s m) -> (b s) m", s=16)
            sp.dma_start(flat(O[oname], j * CHUNK_ROWS), flat(A[name], NQ + j * CHUNK_ROWS)).then_inc(copied, 16)

        def head_of(ap, b, r0, n, h, pat, **kw):
            v = ap[b, r0:r0 + n]
            v = v[:, h:h + 1, :] if isinstance(h, int) else v[:, bass.ds(h, 1), :]
            return v.rearrange(pat, **kw)

        def load_near(name, dst, b, h, s):
            near = head_of(A[name], b, PAST - NEAR, NEAR, h, "(p j) h d -> p j (h d)", j=4)
            sp.dma_start(dst[:, 0:4, :], near).then_inc(s, 16)

        def load_far(name, dst, b, h, s):
            far = head_of(A[name], b, 0, PAST - NEAR, h, "(a r) h d -> a r (h d)", r=16)[:, 0:4, :]
            sp.dma_start(dst[0:FAR, 4:8, :], far).then_inc(s, 16)

        sp.dma_start(GA[:, :], A["g_attn"]).then_inc(ga_in, 16)
        sp.dma_start(ZRAW[:, :, :], A["w_in"].rearrange("(k p) n -> p k n", p=P)[:, :, C_ZA:C_ZA + RANK]).then_inc(za_in, 16)
        for i in range(4):
            sp.dma_start(HB[:, :].rearrange("p (k t) -> p k t", k=KT)[:, 4 * i:4 * i + 4, :],
                         A["x_t"][:, 4 * i:4 * i + 4, :]).then_inc(x_in[i], 16)
        w_in = A["w_in"]
        for c, col in enumerate((C_QB, C_KB, C_VB, C_QB + P, C_KB + P, C_VB + P)):
            load_unit(w_cols(w_in, col), raw3, c)
            if c == 1:
                for dst, name in ((ONES, "ones"), (IDENT, "ident"), (GF, "g_ffn"), (GZ, "g_final"), (GG, "g_gla"), (BG, "b_gate")):
                    sp.dma_start(dst[:, :], A[name]).then_inc(consts_in, 16)
        sp.wait_ge(sums_done, 2)

        def swa_loads(h, hc, it, cols):
            def k_rows(b):
                n = 8 * hc + b - 1
                if n > 0:
                    sp.wait_ge(k_turned, at(n, it, 16))
                load_near("cache_swa_k", KR[b % 2], b, h, k_in[b % 2])
                load_far("cache_swa_k", KR[b % 2], b, h, k_in[b % 2])

            def v_rows(b):
                n = 16 * hc + 2 * (b - 4)
                if b in (2, 3):
                    sp.wait_ge(pv_done, at(hc + 1, it, 2))
                for i, load in enumerate((load_near, load_far)):
                    if n >= 0 and b not in (2, 3):
                        sp.wait_ge(pvs_done, at(n + i + 1, it, 32))
                    load("cache_swa_v", VR[b % 4], b, h, [vnear_in, vfar_in][i][b % 4])
            u = 3 * hc + 6
            for b in range(2):
                k_rows(b)
            for b in range(2):
                v_rows(b)
            load_unit(w_cols(w_in, cols[0]), raw3, u, it, 6)
            for b in range(2, 5):
                k_rows(b)
                if b < 4:
                    v_rows(b)
            load_unit(w_cols(w_in, cols[1]), raw3, u + 1, it, 6)
            for b in range(5, NB):
                k_rows(b)
            for b in range(4, NB):
                v_rows(b)
            load_unit(w_cols(w_in, cols[2]), raw3, u + 2, it, 6)

        def next_cols(h):
            return [h * P + (c + 2 * P) for c in (C_QB, C_KB, C_VB)]
        for h in range(2):
            swa_loads(h, h, None, next_cols(h))
        with sp.Fori(0, 2) as it:
            for hh in range(2):
                h = it * 2 + (2 + hh)
                swa_loads(h, 2 + hh, it, next_cols(h))
        swa_loads(6, 6, None, [C_QA, C_KA, C_VA])
        swa_loads(7, 7, None, [C_VA + P, C_GA, C_GA + P])

        with sp.Fori(0, GH - 1) as it:
            cols = [it * P + (C_QA + P), it * P + (C_KA + P), it * DV + (C_VA + DV),
                    it * DV + (C_VA + DV + P), it * DV + (C_GA + DV), it * DV + (C_GA + DV + P)]
            j = 0
            for i, col in enumerate(cols):
                load_unit(w_cols(w_in, col), raw3, U_GLA + 6 + i, it, 6)
                for _ in range(3 if i < 2 else 2):
                    copy_cache(1, it, j)
                    j += 1
            assert j == COPIES
        w_out = A["w_out"]
        for m in range(3):
            load_unit(w_cols(w_out, m * P), raw3, U_OUT + m)

        def load_x(m, mc, it=None):
            if mc >= 2:
                sp.wait_ge(half_read, at(2 * (U_OUT + mc - 2) + 2, it, 8))
            sp.dma_start(XR[mc % 2][:, :], A["x_t"][:, bass.ds(m, 1), :].rearrange("p o t -> p (o t)")
                         if it is not None else A["x_t"][:, m, :]).then_inc(xr_in[mc % 2], 16)
        sp.wait_ge(la_done, GH)
        load_x(0, 0)
        sp.wait_ge(ss_done, 2 * GH)
        load_x(1, 1)
        sp.wait_ge(mix_done, 2 * GH)
        sp.wait_ge(state_stored, 16 * GH)
        sp.wait_ge(sstate_stored, 16 * GH)
        sp.dma_start(WC[:, :, :], A["w_conv"]).then_inc(conv_in, 16)
        sp.dma_start(BC[:, :], A["b_conv"]).then_inc(conv_in, 16)
        with sp.Fori(0, 3) as it:
            for i in range(4):
                load_unit(w_cols(w_out, it * 4 * P + (3 + i) * P), raw3, U_OUT + 3 + i, it, 4)
                load_x(it * 4 + (2 + i), 2 + i, it)
                for j in range([0, 4, 8, 11][i], [4, 8, 11, 14][i]):
                    copy_cache(0, it, j)
        load_unit(w_cols(w_out, 15 * P), raw3, U_OUT + 15)
        load_x(14, 14)
        load_x(15, 15)

        w_up, w_down = A["w_up"], A["w_down"].rearrange("(n k p) m -> n p k m", k=GT, p=P)
        cin = A["conv_in"].rearrange("p (s n) x -> p s n x", s=2)

        def up_units(g, c, it=None, k=0, after=None):
            for j in range(GT):
                for s in range(2):
                    col = (s * FT + j) * P
                    col = g * (GT * P) + col
                    load_unit(w_cols(w_up, col), raw3, c + 2 * j + s, it, k)
                    if after:
                        after(2 * j + s)

        def down_units(g, c, it=None, k=0, after=None):
            for m in range(DOWN):
                src = w_down[g] if isinstance(g, int) else w_down[bass.ds(g, 1)].rearrange("o p k m -> (o p) k m")
                load_unit(src[:, :, m * 512:(m + 1) * 512], raw4, c + m, it, k)
                if after:
                    after(PAIR + m)

        sp.dma_start(CI[0][:, :, :, :], cin[:, :, 0:GT, :]).then_inc(ci_in[0], 16)
        up_units(0, U_FFN)
        with sp.Fori(0, (NG - 1) // 2) as it:
            for p in range(2):
                c = U_FFN + PAIR + p * (PAIR + DOWN)

                def after(k, p=p):
                    n = p * (PAIR + DOWN) + k
                    if n < COPIES:
                        copy_cache(0, it + 3, n)
                    if n >= 2 * (PAIR + DOWN) - COPIES:
                        copy_cache(1, it + 3, n - (2 * (PAIR + DOWN) - COPIES))
                g = it * 2 + (1 + p)
                sp.wait_ge(conv_done, it * (2 * PAIR) + (PAIR if p else 1))
                sp.dma_start(CI[(1 + p) % 2][:, :, :, :], cin[:, :, bass.ds(g * GT, GT), :]).then_inc(ci_in[(1 + p) % 2], 16)
                up_units(g, c, it, 2 * (PAIR + DOWN), after)
                down_units(it * 2 + p, c + PAIR, it, 2 * (PAIR + DOWN), after)
        down_units(NG - 1, U_FFN + NG * PAIR + (NG - 1) * DOWN)
        for k in range(0, KT, 2):
            sp.wait_ge(y_done, k + 2)
            sp.dma_start(O["y_t"][:, k:k + 2, :], HB[:, k * T:(k + 2) * T].rearrange("p (k t) -> p k t", k=2)).then_inc(out_stored, 16)
        sp.wait_ge(out_stored, 16 * (KT // 2))
        sp.wait_ge(copied, 16 * 2 * NB * COPIES)

    @block.tensor
    def _(pe):
        def mm3(out, w_h, w_l, x_h, x_l, first, last):
            pe.matmul(out, w_h, x_h, start=first, stop=False)
            pe.matmul(out, w_h, x_l, start=False, stop=False)
            return pe.matmul(out, w_l, x_h, start=False, stop=last)

        def sums(src, banks=PJ):
            for x in range(2):
                ins = pe.matmul(banks[x][:, 0:HALF], ONES[:, :], src[:, x * HALF:(x + 1) * HALF], start=True, stop=True)
                ins.then_inc(sums_done, 1)

        def steps(x, c, lo, hi, it=None, k=0):
            if lo == 0 and x == 0:
                pe.wait_ge(lo_done, at(c + 1, it, k))
            if lo == 0 and c >= 1:
                pe.wait_ge(half_read, at(2 * c + x - 1, it, 2 * k))
            s = c % 2
            for kt in range(lo, hi):
                w = slice(kt * P, (kt + 1) * P)
                t = slice(x * HALF, (x + 1) * HALF)
                ins = mm3(PJ[x][:, 0:HALF], WH[s][:, w], WL[s][:, w], XH[:, kt, t], XL[:, kt, t], kt == 0, kt == KT - 1)
            if hi == KT:
                ins.then_inc(half_done, 1)

        def project(x, c, it=None, k=0):
            steps(x, c, 0, KT, it, k)

        def both_halves(banks, c, order, x_h, x_l, ready, lo, hi, done):
            s = c % 2
            for n in range(lo, hi):
                pe.wait_ge(ready, n + 1)
                w = slice(order[n] * P, (order[n] + 1) * P)
                for x in range(2):
                    t = slice(x * HALF, (x + 1) * HALF)
                    ins = mm3(banks[x][:, 0:HALF], WH[s][:, w], WL[s][:, w], x_h[:, order[n], t], x_l[:, order[n], t], n == 0, n == KT - 1)
                    if n == KT - 1:
                        ins.then_inc(done, 1)

        def first_out(lo, hi):
            both_halves(PJ, U_OUT, MIX_ORDER, XH, XL, ml_done, lo, hi, half_done)

        def part(u, lo, hi, it, k):
            while lo < hi:
                x, n = (lo // KT) % 2, lo % KT
                end = min(KT, n + hi - lo)
                steps(x, u + lo // (2 * KT), n, end, it, k)
                lo += end - n

        def turn(out, in_, n):
            return pe.transpose(out, in_, IDENT[0:n, 0:n])

        pe.wait_ge(zs_done, 2)
        for k in range(KT):
            pe.wait_ge(xl_done, k + 1)
            for x in range(2):
                t = slice(x * HALF, (x + 1) * HALF)
                pe.matmul([SA, SB][x][0:2 * SAMP, 0:HALF], ZZ[:, k, :], XH[:, k, t], start=k == 0, stop=False, skip_group_check=True)
                ins = pe.matmul([SA, SB][x][0:RANK, 0:HALF], ZZ[:, k, 0:RANK], XL[:, k, t], start=False, stop=k == KT - 1, skip_group_check=True)
                if k == KT - 1:
                    ins.then_inc(za_half, 1)
        project(0, 0)
        pe.wait_ge(consts_in, 16 * 6)
        pe.wait_ge(acc_done, 1)
        sums(ACC, (T0, T1))
        project(1, 0)
        for u in range(1, 3):
            project(0, u)
            project(1, u)

        def swa_head(hc, it):
            def n(per, c):
                return at(per * hc + c, it, 2 * per)
            g = GRP[:, hc % 2]
            q, k, v = g[:, 0], g[:, 1], g[:, 2]
            u = 3 * hc + 3
            pe.wait_ge(half_read, n(6, 6))
            for j in range(4):
                turn(T0[:, j * P:(j + 1) * P], v[:, j * P:(j + 1) * P], P)
            turn(T1[0:SAMP, 0:HD], v[:, SEQ:T], P)
            turn(T1[0:SAMP, HD:2 * HD], k[:, SEQ:T], P).then_inc(v_turned, 1)
            part(u, 0, 6, it, 6)
            pe.wait_ge(v_rows_done, n(3, 3))
            pe.wait_ge(pvs_read, n(1, 1))
            for i in range(4):
                pe.matmul([SA, SB, BO, BZ][i][:, 0:(i + 1) * P], q[:, i * P:(i + 1) * P], k[:, 0:(i + 1) * P],
                          start=True, stop=True).then_inc(scores_done, 1)
            part(u, 6, 20, it, 6)
            pe.wait_ge(norm_done, n(4, 4))
            for i in range(4):
                for j in range(i + 1):
                    dst = [SA[:, 0:P], SA[:, P:3 * P], SB[:, 0:3 * P], BO[:, :]][i]
                    ins = turn(dst[:, j * P:(j + 1) * P], SP_[:, POFF[i] + j * P:POFF[i] + (j + 1) * P], P)
            ins.then_inc(probs_turned, 1)

            def turn_keys(b):
                pe.wait_ge(k_in[b % 2], at(32 * (4 * hc + b // 2 + 1), it, 32 * 8))
                for j in range(4):
                    turn(T0[:, j * P:(j + 1) * P], KR[b % 2][:, j, :], P)
                for j in range(4):
                    ins = turn(T1[:, j * FAR:(j + 1) * FAR], KR[b % 2][0:FAR, 4 + j, :], FAR)
                ins.then_inc(k_turned, 1)
            turn_keys(0)
            part(u, 20, 34, it, 6)
            pe.wait_ge(pt_done, n(4, 4))
            for j in range(4):
                ins = pe.matmul(BZ[:, j * P:SEQ], VN[:, j, :], PT[:, j, j * P:SEQ], start=j == 0, stop=j == 3, skip_group_check=True)
            ins.then_inc(pv_done, 1)
            pe.wait_ge(qp_done, n(1, 1))
            for b in range(NB):
                pe.wait_ge(kl_done, n(16, 2 * b + 2))
                both = QP[:, b * 2 * SAMP:(b + 1) * 2 * SAMP]
                high = QP[:, b * 2 * SAMP:b * 2 * SAMP + SAMP]
                for dst, w, rows, cols in ((SA, KTH, both, slice(0, NEAR)), (SB, KTH, both, slice(NEAR, NKEY - SAMP)),
                                           (SA, KTL, high, slice(0, NEAR)), (SB, KTL, high, slice(NEAR, NKEY - SAMP))):
                    m = rows.shape[1]
                    ins = pe.matmul(dst[0:m, 0:cols.stop - cols.start], rows, w[:, cols], start=b == 0 and m > SAMP,
                                    stop=b == NB - 1 and m == SAMP, skip_group_check=True)
                if b == 0:
                    pe.matmul(SB[0:SAMP, 4 * FAR:4 * FAR + SAMP], q[:, SEQ:T], k[:, SEQ:T], start=False, stop=True, skip_group_check=True)
                if b + 1 < NB:
                    turn_keys(b + 1)
                    part(u, 34 + 6 * b, 40 + 6 * b, it, 6)
            ins.then_inc(qk_done, 1)
            part(u, 76, 90, it, 6)
            pe.wait_ge(snorm_done, n(1, 1))
            pe.sem_inc(passed, 1)
            for j in range(4):
                turn(T0[:, j * SAMP:(j + 1) * SAMP], SS[:, j * P:(j + 1) * P], SAMP)
            for j in range(4):
                turn(T0[0:FAR, (4 + j) * SAMP:(5 + j) * SAMP], SS[:, NEAR + j * FAR:NEAR + (j + 1) * FAR], SAMP)
            turn(T0[0:SAMP, 8 * SAMP:9 * SAMP], SS[:, NEAR + 4 * FAR:NKEY], SAMP).then_inc(sprobs_turned, 1)
            part(u, 90, 92, it, 6)
            pe.wait_ge(pts_done, n(3, 3))
            pe.wait_ge(pv_read, n(1, 1))
            for b in range(NB):
                out = BZ[b % 4 * SAMP:(b % 4 + 1) * SAMP, b // 4 * P:(b // 4 + 1) * P]
                for j in range(8):
                    if j % 4 == 0:
                        pe.wait_ge([vnear_in, vfar_in][j // 4][b % 4], at(16 * (2 * hc + b // 4 + 1), it, 16 * 4))
                    rows = P if j < 4 else FAR
                    ins = pe.matmul(out, PTS[0:rows, j, :], VR[b % 4][0:rows, j, :], start=j == 0, stop=j == 7, skip_group_check=True)
                    if j % 4 == 3:
                        ins.then_inc(pvs_done, 1)
                if b == 3:
                    part(u, 92, 94, it, 6)
            part(u, 94, 96, it, 6)
            pe.matmul(BO[:, 0:SAMP], VN[0:SAMP, 4, :], PTS[0:SAMP, 8, :], start=True, stop=True)
            pe.wait_ge(ot_done, n(1, 1))
            for w in range(2):
                ins = turn(BO[:, (w + 1) * P:(w + 2) * P], OT[:, w, :], P)
            ins.then_inc(ot_turned, 1)
        with pe.Fori(0, HEADS // 2) as it:
            for hh in range(2):
                swa_head(hh, it)

        def gla_head(it, c, last):
            def n(per, d):
                return at(per * c + d, it, per)
            u = U_GLA + 3 + 6 * c
            g0, g1 = GRP[:, 0], GRP[:, 1]
            pe.wait_ge(wg_in, n(16, 16))
            pe.wait_ge(za_done, 2)
            pe.wait_ge(half_read, at(2 * u, it, 12))
            pe.matmul(T0[:, 0:SEQ], WG[:, :], ZA[:, 0:SEQ], start=True, stop=True)
            pe.matmul(T1[:, 0:SAMP], WG[:, :], ZA[:, SEQ:T], start=True, stop=True).then_inc(z_done, 1)
            project(0, u, it, 6)
            project(1, u, it, 6)

            def turn_v(src):
                for j in range(4):
                    turn(BO[:, j * P:(j + 1) * P], src[:, j * P:(j + 1) * P], P)
                turn(T1[0:SAMP, 0:P], src[:, SEQ:T], P).then_inc(gv_turned, 1)
            pe.wait_ge(z_read, n(2, 2))
            turn_v(g0[:, 2])
            project(0, u + 1, it, 6)
            pe.wait_ge(kd_done, n(1, 1))
            pe.wait_ge(qd_done, n(1, 1))
            for j in range(4):
                t = slice(j * P, (j + 1) * P)
                pe.matmul(SA[:, t], KD[:, t], QD[:, t], start=True, stop=True)
            pe.matmul(SB[0:SAMP, 0:SAMP], KD[:, SEQ:T], QD[:, SEQ:T], start=True, stop=True).then_inc(at_done, 1)
            pe.wait_ge(ke_done, n(1, 1))
            pe.wait_ge(gv_done, n(4, 2))
            for j in range(4):
                turn(T0[:, j * P:(j + 1) * P], g0[:, 1, j * P:(j + 1) * P], P)
            turn(T1[0:SAMP, 0:P], g0[:, 1, SEQ:T], P).then_inc(kn_turned, 1)
            project(1, u + 1, it, 6)
            pe.wait_ge(kn_done, n(2, 2))
            pe.wait_ge(half_read, at(2 * u + 2, it, 12))
            turn_v(g1[:, 0])
            project(0, u + 2, it, 6)
            pe.wait_ge(gv_done, n(4, 4))
            for ch in range(NCH):
                rows = slice((ch % 2) * CH, (ch % 2 + 1) * CH)
                ins = pe.matmul(addition(ch), KN[rows, ch // 2, :], GVN[rows, ch // 2, :],
                                start=True, stop=True)
            ins.then_inc(inc_done, 1)
            project(1, u + 2, it, 6)
            if not last:
                project(0, u + 3, it, 6)
            pe.wait_ge(at_read, n(2, 2))
            pe.wait_ge(state_done, n(8, 8))
            for w in range(2):
                o_ = [SA, SB][w]
                dv = slice(w * P, (w + 1) * P)
                for j in range(4):
                    t = slice(j * P, (j + 1) * P)
                    pe.matmul(o_[:, t], GVN[:, j, dv], AT[:, t], start=j == 0, stop=True, skip_group_check=True)
                for ch in range(1, NCH):
                    t = slice(ch * CH, (ch + 1) * CH)
                    pe.matmul(o_[:, t], ST[:, ch - 1, dv], QD[:, t], start=False, stop=True, skip_group_check=True)
            for w in range(2):
                pe.matmul(T0[:, w * SAMP:(w + 1) * SAMP], GVN[0:SAMP, 4, w * P:(w + 1) * P], AT[0:SAMP, SEQ:T], start=True, stop=True)
            pe.wait_ge(s0_in, n(16, 16))
            for b in range(NB):
                ins = pe.matmul(BZ[b % 4 * SAMP:(b % 4 + 1) * SAMP, b // 4 * DV:(b // 4 + 1) * DV], QD[:, SEQ:T], S0[:, b, :],
                                start=True, stop=True, skip_group_check=True)
            ins.then_inc(o_done, 1)
            if not last:
                steps(1, u + 3, 0, 6, it, 6)
            else:
                pe.wait_ge(lo_done, U_OUT + 1)
                pe.wait_ge(half_read, 2 * U_OUT)
                first_out(0, 3)
            pe.wait_ge(or_done, n(1, 1))
            for w in range(2):
                for m in range(2):
                    ins = turn([T1, BO][w][:, m * P:(m + 1) * P], OR[:, m * DV + w * P:m * DV + (w + 1) * P], P)
            ins.then_inc(or_turned, 1)
            if not last:
                steps(1, u + 3, 6, KT, it, 6)
            else:
                first_out(3, 6)
            pe.wait_ge(os_done, n(1, 1))

            def sample_adds(i):
                pe.wait_ge(vm_done, n(2, i + 1))
                for b in range(4):
                    dst = [T1, BO][b // 2]
                    ins = pe.matmul(dst[:, (b % 2) * DV:(b % 2 + 1) * DV], KN[0:SAMP, 4, :], VM[:, b, :], start=True, stop=True)
                ins.then_inc(us_done, 1)
            sample_adds(0)
            pe.wait_ge(sq2_done, n(1, 1))
            pe.matmul(BZ[:, 0:SEQ], ONES[:, :], EA[:, 0:SEQ], start=True, stop=True)
            pe.matmul(T0[:, 0:SAMP], ONES[:, :], EA[:, SEQ:T], start=True, stop=True).then_inc(gsum_done, 1)
            if not last:
                project(0, u + 4, it, 6)
            else:
                first_out(6, READY)
            pe.wait_ge(ss_done, n(2, 1))
            sample_adds(1)
            if not last:
                project(1, u + 4, it, 6)
                project(0, u + 5, it, 6)
                project(1, u + 5, it, 6)
        with pe.Fori(0, GH - 1) as it:
            gla_head(it, 0, False)
        gla_head(None, GH - 1, True)

        first_out(READY, KT)
        project(0, U_OUT + 1)
        project(1, U_OUT + 1)
        with pe.Fori(0, 7) as it:
            for i in range(2):
                project(0, U_OUT + 2 + i, it, 2)
                project(1, U_OUT + 2 + i, it, 2)

        def up(c, f, it=None):
            for x in range(2):
                n = f + x
                if x == 0:
                    pe.wait_ge(lo_done, at(c + 1, it, 24))
                if n >= 8:
                    pe.wait_ge(fhalf_read, at(n - 7, it, 96))
                s = c % 2
                for kt in range(KT):
                    w = slice(kt * P, (kt + 1) * P)
                    t = slice(x * HALF, (x + 1) * HALF)
                    ins = mm3(bank[n % 8][:, 0:HALF], WH[s][:, w], WL[s][:, w], XH[:, kt, t], XL[:, kt, t], kt == 0, kt == KT - 1)
                ins.then_inc(fhalf_done, 1)

        def down(c, f, gpar, acts, it=None):
            pe.wait_ge(lo_done, at(c + 1, it, 24))
            pe.wait_ge(al_done, at(acts, it, 2 * GT))
            s = c % 2
            for j in range(4):
                for x in range(2):
                    n = f + 2 * j + x
                    pe.wait_ge(fhalf_read, at(n - 7, it, 96))
                    for kt in range(GT):
                        w = slice(kt * 512 + j * P, kt * 512 + (j + 1) * P)
                        t = slice(x * HALF, (x + 1) * HALF)
                        ins = mm3(bank[n % 8][:, 0:HALF], WH[s][:, w], WL[s][:, w], AH[gpar][:, kt, t], AL[gpar][:, kt, t], kt == 0, kt == GT - 1)
                    ins.then_inc(fhalf_done, 1)
        pe.wait_ge(lo_done, U_FFN + 1)
        both_halves(bank, U_FFN, range(KT), XH, XL, fl_done, 0, KT, fhalf_done)
        pe.wait_ge(acc_done, 1 + KT)
        sums(ACC)
        for i in range(1, PAIR):
            up(U_FFN + i, 2 * i)
        c0, f0 = U_FFN + PAIR, 2 * PAIR
        with pe.Fori(0, (NG - 1) // 2) as it:
            for p in range(2):
                c, f = c0 + p * (PAIR + DOWN), f0 + p * 48
                for i in range(PAIR):
                    up(c + i, f + 2 * i, it)
                for i in range(DOWN):
                    down(c + PAIR + i, f + 16 + 8 * i, p, GT * (p + 1), it)
        c, f = U_FFN + NG * PAIR + (NG - 1) * DOWN, f0 + (NG - 1) * 48
        for i in range(DOWN):
            down(c + i, f + 8 * i, 0, GT * NG)
        pe.wait_ge(acc_done, 1 + 2 * KT)
        pe.wait_ge(fhalf_read, f + 8 * DOWN)
        sums(ACC)

    @block.scalar
    def _(act):
        own = Order(act, act_own)

        def hi(c, it=None, k=0, ffn=None):
            act.wait_ge(raw_ready[c % 2], at(16 * (c // 2 + 1), it, 8 * k))
            if ffn is not None:
                act.wait_ge(fhalf_done, at(ffn, it, 96))
            elif c >= 2:
                act.wait_ge(half_done, at(2 * c - 2, it, 2 * k))
            act.activation(WH[c % 2][:, :], RAW[c % 2][:, :], ACT.Copy).then_inc(hi_done, 1)

        def square(lo_, hi_):
            for k in range(lo_, hi_):
                act.wait_ge(xl_done, k + 1)
                act.activation(hb(k), hb(k), ACT.Square).then_inc(sq_done, 1)
        act.wait_ge(za_in, 16)
        act.wait_ge(qp_zero, 2)
        act.activation(ZZ[:, :, 0:RANK], ZRAW[:, :, :], ACT.Copy).then_inc(zs_done, 1)
        act.wait_ge(ga_in, 16)
        for i in range(4):
            act.wait_ge(x_in[i], 16)
            for k in range(4 * i, 4 * i + 4):
                act.activation(XH[:, k, :], hb(k), ACT.Copy, scale=GA[:, k:k + 1]).then_inc(xh_done, 1)
            square(SQUARED[i], SQUARED[i + 1])
        hi(0)
        square(SQUARED[4], KT)
        hi(1)
        act.wait_ge(ms_done, 2)
        act.activation(RN[:, :], RN[:, :], ACT.Sqrt).then_inc(sqrt_done, 1)
        hi(2)
        hi(3)

        def swa_head(hc, it):
            def n(per, c):
                return at(per * hc + c, it, 2 * per)
            u = 3 * hc + 3
            hi(u + 1, it, 6)
            act.wait_ge(v_turned, n(1, 1))
            act.wait_ge(rows_free, n(1, 1))
            act.activation(VN[:, 0:4, :], T0[:, :].rearrange("p (j d) -> p j d", j=4), ACT.Copy).then_inc(v_rows_done, 1)
            act.activation(VN[0:SAMP, 4, :], T1[0:SAMP, 0:HD], ACT.Copy).then_inc(v_rows_done, 1)
            act.activation(KNEW[:, :], T1[0:SAMP, HD:2 * HD], ACT.Copy).then_inc(v_rows_done, 1)
            for i in range(4):
                act.wait_ge(max_done, n(4, i + 1))
                s = SP_[:, POFF[i]:POFF[i] + (i + 1) * P]
                act.activation(s, s, ACT.Exp, bias=SM[:, 4 + i:5 + i], scale=1.0, accum_out=SM[:, 8 + i:9 + i]).then_inc(exp_done, 1)
            h = HEADS + hc if it is None else it * 2 + (HEADS + hc)
            for b in range(NB):
                act.wait_ge(k_turned, n(8, b + 1))
                act.activation(KTH[:, 0:NEAR], T0[:, 0:NEAR], ACT.Copy).then_inc(kh_done, 1)
                act.activation(KTH[:, NEAR:NEAR + 4 * FAR], T1[:, 0:4 * FAR], ACT.Copy).then_inc(kh_done, 1)
                if b == 0:
                    act.wait_ge(pv_done, n(1, 1))
                    act.activation(hb(h, 0, SEQ), BZ[:, 0:SEQ], ACT.Copy).then_inc(pv_read, 1)
                    hi(u + 2, it, 6)
            act.wait_ge(smax_done, n(1, 1))
            act.activation(SS[:, :], SS[:, :], ACT.Exp, bias=SM[0:SAMP, 15:16], scale=1.0, accum_out=SM[0:SAMP, 16:17]).then_inc(sexp_done, 1)
            hi(u + 3, it, 6)
            act.wait_ge(pvs_done, n(16, 16))
            act.activation(OT[:, :, :], BZ[:, 0:2 * P].rearrange("p (w d) -> p w d", w=2), ACT.Copy).then_inc(ot_done, 1)
        with act.Fori(0, HEADS // 2) as it:
            for hh in range(2):
                swa_head(hh, it)

        act.wait_ge(scratch_free, 1)
        act.wait_ge(gconst_in, 16 * 4)

        def mixed_high(lo, hi):
            act.wait_ge(half_done, 2 * U_OUT)
            if hi > 8:
                act.wait_ge(mix_done, hi - 8)
            for k in MIX_ORDER[lo:hi]:
                act.activation(XH[:, k, :], hb(k), ACT.Copy).then_inc(mh_done, 1)

        def gla_head(it, c, last):
            def n(per, d):
                return at(per * c + d, it, per)
            u = U_GLA + 3 + 6 * c
            g = GRP[:, 1]
            act.wait_ge(z_done, n(1, 1))
            bg = BG[:, c:c + 1] if it is None else BG[:, bass.ds(it, 1)]
            act.activation(LA[:, 0:SEQ], T0[:, 0:SEQ], ACT.Identity, bias=bg).then_inc(z_read, 1)
            act.activation(LA[:, SEQ:T], T1[:, 0:SAMP], ACT.Identity, bias=bg).then_inc(z_read, 1)
            act.wait_ge(z_read, n(2, 2))
            own.mark(act.activation(EA[:, :], LA[:, :], ACT.Abs))
            own.wait()
            own.mark(act.activation(EB[:, :], EA[:, :], ACT.Exp, scale=-1.0))
            own.wait()
            act.activation(EA[:, :], EB[:, :], ACT.Ln, bias=1.0).then_inc(e_done, 1)
            hi(u + 1, it, 6)
            act.wait_ge(la_done, n(1, 1))
            act.activation(EB[:, :], LA[:, :], ACT.Exp, scale=1.0 / TAU).then_inc(e_done, 1)
            act.activation(EA[:, :], LA[:, :], ACT.Exp, scale=-1.0 / TAU).then_inc(e_done, 1)
            own.mark(act.activation(ET[:, 0:NCH], LA[:, 0:SEQ].rearrange("p (c t) -> p c t", t=CH)[:, :, CH - 1], ACT.Exp, scale=1.0 / TAU))
            act.activation(ET[:, 8:16], samples(LA[:, SEQ:T])[:, :, NQ - 1], ACT.Exp, scale=1.0 / TAU).then_inc(e_done, 1)
            act.wait_ge(dt_done, n(2, 2))
            act.activation(EB[:, :], EB[:, :], ACT.Exp, scale=1.0 / TAU).then_inc(e_done, 1)

            def v_rows(w):
                act.wait_ge(gv_turned, n(2, w + 1))
                dv = slice(w * P, (w + 1) * P)
                act.activation(GVN[:, 0:4, dv], BO[:, :].rearrange("p (j d) -> p j d", j=4), ACT.Copy).then_inc(gv_done, 1)
                act.activation(GVN[0:SAMP, 4, dv], T1[0:SAMP, 0:P], ACT.Copy).then_inc(gv_done, 1)
            v_rows(0)
            hi(u + 2, it, 6)
            act.wait_ge(kn_turned, n(1, 1))
            act.activation(KN[:, 0:4, :], T0[:, :].rearrange("p (j d) -> p j d", j=4), ACT.Copy).then_inc(kn_done, 1)
            act.activation(KN[0:SAMP, 4, :], T1[0:SAMP, 0:P], ACT.Copy).then_inc(kn_done, 1)
            v_rows(1)
            hi(u + 3, it, 6)
            act.wait_ge(half_read, at(2 * u + 6, it, 12))
            for w in range(2):
                act.activation(g[:, 1 + w, :], g[:, 1 + w, :], ACT.Silu).then_inc(silu_done, 1)
            if last:
                mixed_high(0, 8)
            else:
                hi(u + 4, it, 6)
            act.wait_ge(o_done, n(1, 1))
            act.activation(OR[:, 0:2 * DV], BZ[:, :], ACT.Copy).then_inc(or_done, 1)
            act.activation(EA[:, 0:SEQ], SA[:, 0:SEQ], ACT.Square).then_inc(sqg_done, 1)
            act.activation(EB[:, 0:SEQ], SB[:, 0:SEQ], ACT.Square).then_inc(sqg_done, 1)
            act.wait_ge(os_done, n(1, 1))
            act.activation(EA[:, SEQ:T], OS[:, 0, :], ACT.Square).then_inc(sqg_done, 1)
            act.activation(EB[:, SEQ:T], OS[:, 1, :], ACT.Square).then_inc(sqg_done, 1)
            if last:
                mixed_high(8, READY)
                hi(u + 4, it, 6)
            if not last:
                hi(u + 5, it, 6)
            act.wait_ge(gms_done, n(2, 2))
            act.activation(EB[:, :], EB[:, :], ACT.Sqrt).then_inc(gsqrt_done, 1)
            if not last:
                hi(u + 6, it, 6)
        with act.Fori(0, GH - 1) as it:
            own.enter(it, 3)
            gla_head(it, 0, False)
            own.leave(GH - 1)
        gla_head(None, GH - 1, True)

        act.wait_ge(mix_done, 2 * GH)
        mixed_high(READY, KT)

        def out_step(c, it=None, k=0):
            m = c - U_OUT
            if m:
                hi(c + 1, it, k)
            act.wait_ge(half_read, at(2 * c + 2, it, 2 * k))
            if m:
                act.wait_ge(acc_done, at(m + 1, it, k))
            else:
                act.wait_ge(state_stored, 16 * GH)
                act.wait_ge(sstate_stored, 16 * GH)
            act.activation(SQ[:, :], hb(m if it is None else it * k + m), ACT.Square).then_inc(hsq_done, 1)
        out_step(U_OUT)
        out_step(U_OUT + 1)
        with act.Fori(0, 7) as it:
            for i in range(2):
                out_step(U_OUT + 2 + i, it, 2)

        for k in range(KT):
            act.activation(XH[:, k, :], hb(k), ACT.Copy, scale=GF[:, k:k + 1]).then_inc(fh_done, 1)

        def used(c):
            if c < PAIR:
                return 2 * (c + 1)
            r, i = divmod(c - PAIR, PAIR + DOWN)
            return 16 + 48 * r + (2 * (i + 1) if i < PAIR else 16 + 8 * (i - PAIR + 1))

        def next_hi(c, it=None):
            i = c - U_FFN
            if i == 0:
                act.wait_ge(raw_ready[(c + 1) % 2], 16 * ((c + 1) // 2 + 1))
                act.wait_ge(half_done, 2 * U_FFN)
                act.activation(WH[(c + 1) % 2][:, :], RAW[(c + 1) % 2][:, :], ACT.Copy).then_inc(hi_done, 1)
            else:
                hi(c + 1, it, 24, ffn=used(i - 1))

        def up_post(g, gc, j, s, f, it=None):
            t = 2 * (GT * gc + j) + s
            act.wait_ge(fhalf_read, at(f + 2, it, 96))
            U, C = (UA, CA) if s == 0 else (UV, CV)
            tile = g * GT + (s * FT + j)
            w2 = WC[:, 2, tile:tile + 1] if it is None else WC[:, 2, bass.ds(tile, 1)]
            b = BC[:, tile:tile + 1] if it is None else BC[:, bass.ds(tile, 1)]
            if it is not None or gc * GT + j >= 1:
                act.wait_ge(prod_done, at(2 * (gc * GT + j), it, 16))
            act.activation(C[:, :], U[:, 2:UW], ACT.Identity, scale=w2, bias=b).then_inc(aff_done, 1)
            if s:
                act.wait_ge(conv_done, at(t, it, 16))
                act.activation(CA[:, :], CA[:, :], ACT.Silu).then_inc(silu2_done, 1)
                act.wait_ge(prod_done, at(2 * (gc * GT + j) + 2, it, 16))
                act.activation(AH[gc % 2][:, j, :], PR[:, :], ACT.Copy).then_inc(ah_done, 1)

        act.wait_ge(conv_in, 32)
        next_hi(U_FFN)
        act.wait_ge(ms_done, 4)
        act.activation(RN[:, :], RN[:, :], ACT.Sqrt).then_inc(sqrt_done, 1)
        for j in range(GT):
            for s in range(2):
                if j or s:
                    next_hi(U_FFN + 2 * j + s)
                up_post(0, 0, j, s, 2 * (2 * j + s))
        c0, f0 = U_FFN + PAIR, 2 * PAIR
        with act.Fori(0, (NG - 1) // 2) as it:
            for p in range(2):
                c, f = c0 + p * (PAIR + DOWN), f0 + p * 48
                for j in range(GT):
                    for s in range(2):
                        next_hi(c + 2 * j + s, it)
                        up_post(it * 2 + (1 + p), 1 + p, j, s, f + 2 * (2 * j + s), it)
                for i in range(DOWN):
                    next_hi(c + PAIR + i, it)
        c = U_FFN + NG * PAIR + (NG - 1) * DOWN
        for i in range(DOWN):
            if i < DOWN - 1:
                next_hi(c + i)
            for j in range(4):
                m = 4 * i + j
                act.wait_ge(fhalf_read, f0 + (NG - 1) * 48 + 2 * m + 2)
                act.wait_ge(acc_done, 1 + KT + m)
                act.activation(SQ[:, :], hb(m), ACT.Square).then_inc(hsq_done, 1)
        act.wait_ge(ms_done, 6)
        act.activation(RN[:, :], RN[:, :], ACT.Sqrt).then_inc(sqrt_done, 1)

    @block.vector
    def _(dve):
        own = Order(dve, dve_own)

        def lo(c, it=None, k=0):
            dve.wait_ge(hi_done, at(c + 1, it, k))
            dve.tensor_tensor(WL[c % 2][:, :], RAW[c % 2][:, :], WH[c % 2][:, :].bitcast(F32), ALU.subtract).then_inc(lo_done, 1)

        def mean_inv(rn_n, banks=PJ):
            dve.wait_ge(sums_done, 2 * rn_n)
            for x in range(2):
                dve.tensor_scalar(RN[:, x * HALF:(x + 1) * HALF], banks[x][:, 0:HALF], 1.0 / D, EPS, ALU.mult, ALU.add).then_inc(ms_done, 1)
            dve.wait_ge(sqrt_done, rn_n)
            dve.reciprocal(RN[:, :], RN[:, :]).then_inc(rn_done, 1)
            dve.wait_ge(rn_done, rn_n)

        def read_half(dst, x, scale, c, it=None, k=0):
            dve.wait_ge(half_done, at(2 * c + x + 1, it, 2 * k))
            t = slice(x * HALF, (x + 1) * HALF)
            dve.scalar_tensor_tensor(dst[:, t], PJ[x][:, 0:HALF], scale, RN[:, t], ALU.mult, ALU.mult).then_inc(half_read, 1)

        def add_squares(lo_, hi_):
            for k in range(max(lo_, 1), hi_):
                dve.wait_ge(sq_done, k + 1)
                if k > 1:
                    own.wait()
                ins = dve.tensor_tensor(ACC[:, :], hb(0) if k == 1 else ACC[:, :], hb(k), ALU.add)
                if k == KT - 1:
                    ins.then_inc(acc_done, 1)
                else:
                    own.mark(ins)
        dve.wait_ge(zs_done, 1)
        dve.tensor_tensor(ZZ[:, :, SAMP:SAMP + RANK], ZRAW[:, :, :], ZZ[:, :, 0:RANK].bitcast(F32), ALU.subtract).then_inc(zs_done, 1)
        dve.wait_ge(ga_in, 16)
        for i in range(4):
            for k in range(4 * i, 4 * i + 4):
                dve.wait_ge(xh_done, k + 1)
                dve.scalar_tensor_tensor(XL[:, k, :], hb(k), GA[:, k:k + 1], XH[:, k, :].bitcast(F32), ALU.mult, ALU.subtract).then_inc(xl_done, 1)
            add_squares(SQUARED[i], SQUARED[i + 1])
        lo(0)
        add_squares(SQUARED[4], KT)
        lo(1)
        mean_inv(1, (T0, T1))
        for u in range(3):
            read_half(GRP[:, 0, u], 0, SCALE if u == 0 else 1.0, u)
            read_half(GRP[:, 0, u], 1, SCALE if u == 0 else 1.0, u)
            if u < 2:
                lo(u + 2)
            if u == 0:
                dve.wait_ge(za_half, 2)
                for x in range(2):
                    t = slice(x * HALF, (x + 1) * HALF)
                    own.mark(dve.tensor_copy(ZA[:, t], [SA, SB][x][SAMP:SAMP + RANK, 0:HALF]))
                    own.wait()
                    own.mark(dve.tensor_tensor(ZA[:, t], [SA, SB][x][0:RANK, 0:HALF], ZA[:, t], ALU.add))
                    own.wait()
                    dve.tensor_tensor(ZA[:, t], ZA[:, t], RN[0:RANK, t], ALU.mult).then_inc(za_done, 1)

        def swa_head(hc, it):
            def n(per, c):
                return at(per * hc + c, it, 2 * per)
            u = 3 * hc + 3
            g = GRP[:, 1 - hc % 2]
            lo(u + 1, it, 6)
            dve.wait_ge(tabp_in, n(16, 16))
            for i in range(4):
                w = (i + 1) * P
                s = SP_[:, POFF[i]:POFF[i] + w]
                dve.wait_ge(scores_done, n(4, i + 1))
                dve.sem_inc(passed, 1)
                own.mark(dve.tensor_tensor_reduce(s, [SA, SB, BO, BZ][i][:, 0:w], TABP[:, SEQ - w:SEQ], 1.0, NEG, ALU.add, ALU.max, SM[:, i:i + 1]))
                own.wait()
                dve.tensor_scalar(SM[:, 4 + i:5 + i], SM[:, i:i + 1], -1.0, None, ALU.mult).then_inc(max_done, 1)
            for i in range(4):
                s = SP_[:, POFF[i]:POFF[i] + (i + 1) * P]
                dve.wait_ge(exp_done, n(4, i + 1))
                own.mark(dve.reciprocal(SM[:, 18 + i:19 + i], SM[:, 8 + i:9 + i]))
                own.wait()
                dve.tensor_scalar(s, s, SM[:, 18 + i:19 + i], None, ALU.mult).then_inc(norm_done, 1)
            dve.wait_ge(rows_free, n(1, 1))
            read_half(g[:, 0], 0, SCALE, u, it, 6)
            dve.wait_ge(probs_turned, n(1, 1))
            for i in range(4):
                src = [SA[:, 0:P], SA[:, P:3 * P], SB[:, 0:3 * P], BO[:, :]][i]
                dve.tensor_copy(PT[:, 0:i + 1, i * P:(i + 1) * P], src.rearrange("p (j t) -> p j t", t=P)).then_inc(pt_done, 1)
            for b in range(NB):
                for i, (bank_, cols) in enumerate(((T0, slice(0, NEAR)), (T1, slice(NEAR, NKEY - SAMP)))):
                    dve.wait_ge(kh_done, n(16, 2 * b + i + 1))
                    dve.tensor_tensor(KTL[:, cols], bank_[:, 0:cols.stop - cols.start], KTH[:, cols].bitcast(F32), ALU.subtract).then_inc(kl_done, 1)
                if b == 0:
                    read_half(g[:, 0], 1, SCALE, u, it, 6)
                elif b == 1:
                    lo(u + 2, it, 6)
                elif b == 3:
                    read_half(g[:, 1], 0, 1.0, u + 1, it, 6)
                elif b == 5:
                    read_half(g[:, 1], 1, 1.0, u + 1, it, 6)
            dve.wait_ge(qk_done, n(1, 1))
            dve.wait_ge(tabs_in, n(16, 16))
            own.mark(dve.tensor_tensor(SS[:, 0:NEAR], SA[SAMP:2 * SAMP, 0:NEAR], TABS[:, 0:NEAR], ALU.add))
            own.mark(dve.tensor_tensor(SS[:, NEAR:NKEY - SAMP], SB[SAMP:2 * SAMP, 0:4 * FAR], TABS[:, NEAR:NKEY - SAMP], ALU.add))
            own.mark(dve.tensor_copy(SS[:, NKEY - SAMP:NKEY], TABS[:, NKEY - SAMP:NKEY]))
            own.wait()
            dve.sem_inc(passed, 1)
            own.mark(dve.tensor_tensor_reduce(SS[:, 0:NEAR], SA[0:SAMP, 0:NEAR], SS[:, 0:NEAR], 1.0, NEG, ALU.add, ALU.max, SM[0:SAMP, 13:14]))
            own.mark(dve.tensor_tensor_reduce(SS[:, NEAR:NKEY], SB[0:SAMP, 0:NKEY - NEAR], SS[:, NEAR:NKEY], 1.0, NEG, ALU.add, ALU.max, SM[0:SAMP, 14:15]))
            own.wait()
            own.mark(dve.tensor_tensor(SM[0:SAMP, 13:14], SM[0:SAMP, 13:14], SM[0:SAMP, 14:15], ALU.max))
            own.wait()
            dve.tensor_scalar(SM[0:SAMP, 15:16], SM[0:SAMP, 13:14], -1.0, None, ALU.mult).then_inc(smax_done, 1)
            dve.wait_ge(sexp_done, n(1, 1))
            own.mark(dve.reciprocal(SM[0:SAMP, 17:18], SM[0:SAMP, 16:17]))
            own.wait()
            dve.tensor_scalar(SS[:, :], SS[:, :], SM[0:SAMP, 17:18], None, ALU.mult).then_inc(snorm_done, 1)
            read_half(g[:, 2], 0, 1.0, u + 2, it, 6)
            dve.wait_ge(sprobs_turned, n(1, 1))
            dve.tensor_copy(PTS[:, 0:4, :], T0[:, 0:4 * SAMP].rearrange("p (j t) -> p j t", j=4)).then_inc(pts_done, 1)
            dve.tensor_copy(PTS[0:FAR, 4:8, :], T0[0:FAR, 4 * SAMP:8 * SAMP].rearrange("p (j t) -> p j t", j=4)).then_inc(pts_done, 1)
            dve.tensor_copy(PTS[0:SAMP, 8, :], T0[0:SAMP, 8 * SAMP:9 * SAMP]).then_inc(pts_done, 1)
            lo(u + 3, it, 6)
            read_half(g[:, 2], 1, 1.0, u + 2, it, 6)
            h = HEADS + hc if it is None else it * 2 + (HEADS + hc)
            dve.wait_ge(ot_turned, n(1, 1))
            for w in range(2):
                first = (w + 1) * P + 16 * w
                old = BO[:, first:first + 4 * 36].rearrange("p (b x) -> p b x", x=36)[:, :, 0:NQ]
                own.mark(dve.tensor_copy(samples(hb(h, SEQ + 16 * w, 16)), old))
            own.wait()
            dve.tensor_tensor(hb(h, SEQ, SAMP), hb(h, SEQ, SAMP), BO[:, 0:SAMP], ALU.add).then_inc(pvs_read, 1)
        with dve.Fori(0, HEADS // 2) as it:
            own.enter(it, 34)
            for hh in range(2):
                swa_head(hh, it)
            own.leave(HEADS // 2)

        dve.wait_ge(scratch_free, 1)
        dve.wait_ge(gconst_in, 16 * 4)

        def mixed_low(lo, hi):
            for i in range(lo, hi):
                k = MIX_ORDER[i]
                dve.wait_ge(mh_done, i + 1)
                dve.tensor_tensor(XL[:, k, :], hb(k), XH[:, k, :].bitcast(F32), ALU.subtract).then_inc(ml_done, 1)

        def gla_head(it, c, last):
            def n(per, d):
                return at(per * c + d, it, per)
            u = U_GLA + 3 + 6 * c
            g0, g1 = GRP[:, 0], GRP[:, 1]
            lo(u + 1, it, 6)
            dve.wait_ge(e_done, n(5, 1))
            own.mark(dve.scalar_tensor_tensor(LA[:, :], LA[:, :], 0.0, EA[:, :], ALU.min, ALU.subtract))
            own.wait()
            dve.tensor_tensor_scan(LA[:, :], RESET[:, :], LA[:, :], 0.0, ALU.mult, ALU.add).then_inc(la_done, 1)
            read_half(g1[:, 0], 0, 1.0, u, it, 6)
            dve.wait_ge(e_done, n(5, 2))
            dve.tensor_tensor(QD[:, :], g0[:, 0], EB[:, :], ALU.mult).then_inc(qd_done, 1)
            dve.wait_ge(e_done, n(5, 4))
            dve.wait_ge(qd_done, n(1, 1))

            def left(ap, width):
                v = ap.rearrange("p (c t) -> p c t", t=width)
                return v, v[:, :, width - 1:width]
            v, tot = left(LA[:, 0:SEQ], CH)
            dve.tensor_tensor(EB[:, 0:SEQ].rearrange("p (c t) -> p c t", t=CH), tot.broadcast_to([P, NCH, CH]), v, ALU.subtract).then_inc(dt_done, 1)
            v, tot = left(LA[:, SEQ:T], NQ)
            dve.tensor_tensor(samples(EB[:, SEQ:T]), tot.broadcast_to([P, NB, NQ]), v, ALU.subtract).then_inc(dt_done, 1)
            dve.tensor_tensor(KD[:, :], g0[:, 1], EA[:, :], ALU.mult).then_inc(kd_done, 1)
            read_half(g1[:, 0], 1, 1.0, u, it, 6)
            dve.wait_ge(e_done, n(5, 5))
            dve.wait_ge(kd_done, n(1, 1))
            dve.tensor_tensor(g0[:, 1], g0[:, 1], EB[:, :], ALU.mult).then_inc(ke_done, 1)
            dve.wait_ge(at_done, n(1, 1))
            dve.tensor_tensor(AT[:, 0:SEQ].rearrange("p (j t) -> p j t", t=P), SA[:, :].rearrange("p (j t) -> p j t", t=P),
                              PM[:, :].unsqueeze(1).broadcast_to([P, 4, P]), ALU.mult).then_inc(at_read, 1)
            dve.tensor_tensor(AT[0:SAMP, SEQ:T], SB[0:SAMP, 0:SAMP], SMK[:, :], ALU.mult).then_inc(at_read, 1)
            lo(u + 2, it, 6)
            read_half(g1[:, 1], 0, 1.0, u + 1, it, 6)

            def masked(i):
                for b in range(4):
                    ins = dve.tensor_scalar(VM[:, b, :], GVN[0:SAMP, 4, :], RM[:, 4 * i + b:4 * i + b + 1], None, ALU.mult)
                ins.then_inc(vm_done, 1)
            dve.wait_ge(gv_done, n(4, 4))
            masked(0)
            read_half(g1[:, 1], 1, 1.0, u + 1, it, 6)
            read_half(g1[:, 2], 0, 1.0, u + 2, it, 6)
            lo(u + 3, it, 6)
            dve.wait_ge(state_free, n(1, 1))
            dve.wait_ge(inc_done, n(1, 1))
            for ch in range(NCH):
                add = addition(ch)
                if ch == 0:
                    dve.tensor_copy(ST[:, 0, :], add).then_inc(state_done, 1)
                else:
                    dve.wait_ge(state_done, n(8, ch))
                    dve.scalar_tensor_tensor(ST[:, ch, :], ST[:, ch - 1, :], ET[:, ch:ch + 1], add, ALU.mult, ALU.add).then_inc(state_done, 1)
            read_half(g1[:, 2], 1, 1.0, u + 2, it, 6)
            if not last:
                read_half(g0[:, 0], 0, SCALE, u + 3, it, 6)
            else:
                mixed_low(0, 8)
            dve.wait_ge(or_turned, n(1, 1))
            for w in range(2):
                for m in range(2):
                    first = m * P + 16 * m
                    own.mark(dve.tensor_copy(samples(OS[:, w, 16 * m:16 * m + 16]),
                                             [T1, BO][w][:, first:first + 4 * 36].rearrange("p (b x) -> p b x", x=36)[:, :, 0:NQ]))
            own.wait()
            dve.tensor_tensor(OS[:, :, :], OS[:, :, :], T0[:, 0:2 * SAMP].rearrange("p (w t) -> p w t", w=2), ALU.add).then_inc(os_done, 1)
            dve.wait_ge(sqg_done, n(4, 4))
            dve.tensor_tensor(EA[:, :], EA[:, :], EB[:, :], ALU.add).then_inc(sq2_done, 1)
            if last:
                mixed_low(8, READY)
            lo(u + 4, it, 6)
            if not last:
                read_half(g0[:, 0], 1, SCALE, u + 3, it, 6)

            def sample_states(i):
                dve.wait_ge(us_done, n(2, i + 1))
                for b in range(4):
                    add = [T1, BO][b // 2][:, (b % 2) * DV:(b % 2 + 1) * DV]
                    s = S0[:, 4 * i + b, :]
                    ins = dve.scalar_tensor_tensor(s, s, ET[:, 8 + 4 * i + b:9 + 4 * i + b], add, ALU.mult, ALU.add)
                ins.then_inc(ss_done, 1)
            sample_states(0)
            dve.wait_ge(gsum_done, n(1, 1))
            dve.tensor_scalar(EB[:, 0:SEQ], BZ[:, 0:SEQ], 1.0 / DV, EPS, ALU.mult, ALU.add).then_inc(gms_done, 1)
            dve.tensor_scalar(EB[:, SEQ:T], T0[:, 0:SAMP], 1.0 / DV, EPS, ALU.mult, ALU.add).then_inc(gms_done, 1)
            masked(1)
            dve.wait_ge(gsqrt_done, n(1, 1))
            own.mark(dve.reciprocal(EB[:, :], EB[:, :]))
            own.wait()
            dve.wait_ge(silu_done, n(2, 2))
            for w in range(2):
                if w:
                    dve.wait_ge(mix_done, n(2, 1))
                gg = GG[:, 2 * c + w:2 * c + w + 1] if it is None else GG[:, bass.ds(it * 2 + w, 1)]
                own.mark(dve.scalar_tensor_tensor(EA[:, 0:SEQ], [SA, SB][w][:, 0:SEQ], gg, EB[:, 0:SEQ], ALU.mult, ALU.mult))
                own.mark(dve.scalar_tensor_tensor(EA[:, SEQ:T], OS[:, w, :], gg, EB[:, SEQ:T], ALU.mult, ALU.mult))
                own.wait()
                tile = 2 * c + w if it is None else it * 2 + w
                dve.tensor_tensor(hb(tile), EA[:, :], g1[:, 1 + w, :], ALU.mult).then_inc(mix_done, 1)
            if not last:
                lo(u + 5, it, 6)
                read_half(g0[:, 1], 0, 1.0, u + 4, it, 6)
            sample_states(1)
            if not last:
                read_half(g0[:, 1], 1, 1.0, u + 4, it, 6)
                lo(u + 6, it, 6)
                read_half(g0[:, 2], 0, 1.0, u + 5, it, 6)
                read_half(g0[:, 2], 1, 1.0, u + 5, it, 6)
        with dve.Fori(0, GH - 1) as it:
            own.enter(it, 10)
            gla_head(it, 0, False)
            own.leave(GH - 1)
        gla_head(None, GH - 1, True)

        mixed_low(READY, KT)

        def out_step(c, it=None, k=0):
            m = c - U_OUT
            if m:
                lo(c + 1, it, k)
            for x in range(2):
                if x == 0:
                    dve.wait_ge(xr_in[m % 2], at(16 * (m // 2 + 1), it, 8 * k))
                    if m == 0:
                        dve.wait_ge(mh_done, KT)
                dve.wait_ge(half_done, at(2 * c + x + 1, it, 2 * k))
                dst = hb(m if it is None else it * k + m, x * HALF, HALF)
                t = slice(x * HALF, (x + 1) * HALF)
                dve.tensor_tensor(dst, PJ[x][:, 0:HALF], XR[m % 2][:, t], ALU.add).then_inc(half_read, 1)
        out_step(U_OUT)
        out_step(U_OUT + 1)
        with dve.Fori(0, 7) as it:
            for i in range(2):
                out_step(U_OUT + 2 + i, it, 2)
        for k in range(KT):
            dve.wait_ge(fh_done, k + 1)
            dve.scalar_tensor_tensor(XL[:, k, :], hb(k), GF[:, k:k + 1], XH[:, k, :].bitcast(F32), ALU.mult, ALU.subtract).then_inc(fl_done, 1)

        def up_post(gc, c, j, s, f, it=None, g=None):
            t = 2 * (GT * gc + j) + s
            U, C = (UA, CA) if s == 0 else (UV, CV)
            b0, b1 = bank[f % 8], bank[(f + 1) % 8]
            if it is not None or t >= 2:
                dve.wait_ge(co_ready, at(t - 1, it, 16))
            if j == 0 and s == 0:
                dve.wait_ge(ci_in[gc % 2], at(16 * (gc // 2 + 1), it, 16))
            dve.tensor_copy(U[:, 2 + SEQ:UW].rearrange("p (b x) -> p b x", x=6)[:, :, 0:2],
                            CI[gc % 2][:, s, j, :].rearrange("p (b x) -> p b x", x=2))
            dve.wait_ge(fhalf_done, at(f + 1, it, 96))
            dve.tensor_tensor(U[:, 2:2 + HALF], b0[:, 0:HALF], RN[:, 0:HALF], ALU.mult).then_inc(fhalf_read, 1)
            dve.wait_ge(fhalf_done, at(f + 2, it, 96))
            dve.tensor_tensor(U[:, 2 + HALF:2 + SEQ], b1[:, 0:SEQ - HALF], RN[:, HALF:SEQ], ALU.mult)
            dve.tensor_tensor(U[:, 2 + SEQ:UW].rearrange("p (b x) -> p b x", x=6)[:, :, 2:6], samples(b1[:, SEQ - HALF:HALF]),
                              samples(RN[:, SEQ:T]), ALU.mult).then_inc(fhalf_read, 1)
            dve.wait_ge(aff_done, at(t + 1, it, 16))
            tile = s * FT + j if it is None else g * GT + (s * FT + j)
            w = [WC[:, i, tile:tile + 1] if it is None else WC[:, i, bass.ds(tile, 1)] for i in range(2)]
            own.mark(dve.scalar_tensor_tensor(C[:, :], U[:, 1:UW - 1], w[1], C[:, :], ALU.mult, ALU.add))
            own.wait()
            dve.scalar_tensor_tensor(C[:, :], U[:, 0:UW - 2], w[0], C[:, :], ALU.mult, ALU.add).then_inc(conv_done, 1)
            if s:
                dve.wait_ge(conv_done, at(t + 1, it, 16))
                dve.wait_ge(silu2_done, at(GT * gc + j + 1, it, 8))
                dve.tensor_tensor(PR[:, 0:SEQ], CA[:, 0:SEQ], CV[:, 0:SEQ], ALU.mult).then_inc(prod_done, 1)
                ca, cv = (C_[:, SEQ:CW].rearrange("p (b x) -> p b x", x=6)[:, :, 2:6] for C_ in (CA, CV))
                dve.tensor_tensor(samples(PR[:, SEQ:T]), ca, cv, ALU.mult).then_inc(prod_done, 1)
                dve.wait_ge(prod_done, at(2 * (GT * gc + j) + 2, it, 16))
                dve.wait_ge(ah_done, at(GT * gc + j + 1, it, 8))
                dve.tensor_tensor(AL[gc % 2][:, j, :], PR[:, :], AH[gc % 2][:, j, :].bitcast(F32), ALU.subtract).then_inc(al_done, 1)

        for U in (UA, UV):
            own.mark(dve.memset(U[:, 0:2], 0.0))
        lo(U_FFN + 1)
        mean_inv(2)
        for j in range(GT):
            for s in range(2):
                if j or s:
                    lo(U_FFN + 2 * j + s + 1)
                up_post(0, U_FFN, j, s, 2 * (2 * j + s))
        c0, f0 = U_FFN + PAIR, 2 * PAIR

        def down_post(c, f, m4, nxt, it=None):
            if nxt:
                lo(c + 1, it, 24)
            for j in range(4):
                for x in range(2):
                    n = f + 2 * j + x
                    dve.wait_ge(fhalf_done, at(n + 1, it, 96))
                    d = hb(4 * m4 + j, x * HALF, HALF)
                    dve.tensor_tensor(d, d, bank[n % 8][:, 0:HALF], ALU.add).then_inc(fhalf_read, 1)
        with dve.Fori(0, (NG - 1) // 2) as it:
            own.enter(it, 2 * PAIR)
            for p in range(2):
                c, f = c0 + p * (PAIR + DOWN), f0 + p * 48
                for j in range(GT):
                    for s in range(2):
                        i = 2 * j + s
                        lo(c + i + 1, it, 24)
                        up_post(1 + p, c, j, s, f + 2 * i, it, it * 2 + (1 + p))
                for i in range(DOWN):
                    down_post(c + PAIR + i, f + 16 + 8 * i, i, True, it)
            own.leave((NG - 1) // 2)
        c, f = U_FFN + NG * PAIR + (NG - 1) * DOWN, f0 + (NG - 1) * 48
        for i in range(DOWN):
            down_post(c + i, f + 8 * i, i, i < DOWN - 1)
        mean_inv(3)
        for k in range(KT):
            dve.scalar_tensor_tensor(hb(k), hb(k), GZ[:, k:k + 1], RN[:, :], ALU.mult, ALU.mult).then_inc(y_done, 1)

    @block.gpsimd
    def _(pool):
        def alone():
            pool.sem_inc(passed, 1)
        pool.memset(QP[:, :].bitcast(F32), 0.0).then_inc(qp_zero, 1)
        pool.memset(ZZ[:, :, :].bitcast(F32), 0.0).then_inc(qp_zero, 1)
        pool.wait_ge(qp_zero, 2)
        pool.dma_start(TABP[:, :], A["tab_prompt"][0]).then_inc(tabp_in, 16)
        pool.dma_start(TABS[:, :], A["tab_sample"][0]).then_inc(tabs_in, 16)
        pool.dma_start(RESET[:, :], A["reset"]).then_inc(gconst_in, 16)
        pool.dma_start(PM[:, :], A["pair_mask"]).then_inc(gconst_in, 16)
        pool.dma_start(SMK[:, :], A["sample_mask"]).then_inc(gconst_in, 16)
        pool.dma_start(RM[:, :], A["row_mask"]).then_inc(gconst_in, 16)
        pool.wait_ge(sums_done, 2)
        pool.dma_start(WG[:, :], A["w_gate"][:, 0:DK]).then_inc(wg_in, 16)

        pool.sem_inc(rows_free, 1)
        pool.sem_inc(state_free, 1)
        pool.sem_inc(pvs_read, 1)

        def swa_head(hc, it):
            def n(per, c):
                return at(per * hc + c, it, 2 * per)
            g = GRP[:, hc % 2]
            h = hc if it is None else it * 2 + hc
            pool.wait_ge(half_read, n(6, 2))
            alone()
            qp = QP[:, :].rearrange("p (b x) -> p b x", x=2 * SAMP + NQ)
            pool.tensor_copy(qp[:, :, 0:NQ], samples(g[:, 0, SEQ:T])).then_inc(qp_high, 1)
            pool.wait_ge(qp_high, n(1, 1))
            pool.tensor_tensor(qp[:, :, SAMP:SAMP + NQ], samples(g[:, 0, SEQ:T]), qp[:, :, 0:NQ].bitcast(F32), ALU.subtract).then_inc(qp_done, 1)
            pool.wait_ge(v_rows_done, n(3, 3))
            alone()

            def rows(name):
                v = O[name][:, PAST - NQ:PAST]
                return v[:, :, bass.ds(h, 1), :].rearrange("b i h d -> b i (h d)")
            pool.dma_start(rows("k_sample"), KNEW[:, :]).then_inc(head_stored, 16)
            pool.dma_start(rows("v_sample"), VN[0:SAMP, 4, :]).then_inc(head_stored, 16)
            pool.dma_start(O["v_prompt"].rearrange("(j p) h d -> p j h d", p=P)[:, :, bass.ds(h, 1), :].rearrange("p j h d -> p j (h d)"),
                           VN[:, 0:4, :]).then_inc(head_stored, 16)
            pool.dma_start(O["k_prompt_t"][bass.ds(h, 1)].rearrange("h p t -> (h p) t"), g[:, 1, 0:SEQ]).then_inc(head_stored, 16)
            pool.wait_ge(max_done, n(4, 4))
            alone()
            pool.dma_start(TABP[:, :], A["tab_prompt"][bass.ds(h + 1, 1)].rearrange("h p t -> (h p) t")).then_inc(tabp_in, 16)
            pool.wait_ge(smax_done, n(1, 1))
            alone()
            pool.dma_start(TABS[:, :], A["tab_sample"][bass.ds(h + 1, 1)].rearrange("h p t -> (h p) t")).then_inc(tabs_in, 16)
            pool.wait_ge(head_stored, n(64, 64))
            pool.sem_inc(rows_free, 1)
        with pool.Fori(0, HEADS // 2) as it:
            for hh in range(2):
                swa_head(hh, it)

        pool.wait_ge(head_stored, 64 * HEADS)
        pool.wait_ge(tabp_in, 16 * (HEADS + 1))
        pool.wait_ge(tabs_in, 16 * (HEADS + 1))
        pool.wait_ge(pvs_read, HEADS + 1)
        pool.sem_inc(scratch_free, 1)

        def gla_head(it, c):
            def n(per, d):
                return at(per * c + d, it, per)
            h = c if it is None else it
            src = A["state_gla"][:, bass.ds(h, 1)] if it is not None else A["state_gla"][:, h:h + 1]
            pool.dma_start(S0[:, :, :], src.rearrange("b h p v -> (h p) b v")).then_inc(s0_in, 16)
            if it is not None:
                pool.wait_ge(z_done, n(1, 1))
                alone()
                pool.dma_start(WG[:, :], A["w_gate"][:, bass.ds(h * DK + DK, DK)]).then_inc(wg_in, 16)
            pool.wait_ge(state_done, n(8, 8))
            alone()
            dst = O["state_prompt"][bass.ds(h, 1)] if it is not None else O["state_prompt"][h:h + 1]
            pool.dma_start(dst.rearrange("h p v -> (h p) v"), ST[:, NCH - 1, :]).then_inc(state_stored, 16)
            pool.wait_ge(ss_done, n(2, 2))
            alone()
            dst = O["state_sample"][:, bass.ds(h, 1)] if it is not None else O["state_sample"][:, h:h + 1]
            pool.dma_start(dst.rearrange("b h p v -> (h p) b v"), S0[:, :, :]).then_inc(sstate_stored, 16)
            pool.wait_ge(state_stored, n(16, 16))
            pool.wait_ge(sstate_stored, n(16, 16))
            pool.sem_inc(state_free, 1)
        with pool.Fori(0, GH - 1) as it:
            gla_head(it, 0)
        gla_head(None, GH - 1)

        def add_squares(c, it=None, k=0, first=False):
            pool.wait_ge(hsq_done, at(c + 1, it, k))
            alone()
            if first:
                if c:
                    pool.wait_ge(sums_done, 4)
                pool.tensor_copy(ACC[:, :], SQ[:, :]).then_inc(acc_done, 1)
            else:
                pool.wait_ge(acc_done, at(c + 1, it, k))
                alone()
                pool.tensor_tensor(ACC[:, :], ACC[:, :], SQ[:, :], ALU.add).then_inc(acc_done, 1)
        pool.wait_ge(mix_done, 2 * GH)
        add_squares(0, first=True)
        with pool.Fori(0, KT - 1) as it:
            add_squares(1, it, 1)

        cout = O["conv_out"].rearrange("p (s n) x -> p s n x", s=2)

        def keep_rows(g, gc, f, it=None):
            if gc:
                pool.wait_ge(co_stored, at(16 * gc, it, 32))
                alone()
            for j in range(GT):
                for s in range(2):
                    t = 2 * (GT * gc + j) + s
                    U = UA if s == 0 else UV
                    pool.wait_ge(fhalf_read, at(f + 2 * (2 * j + s) + 2, it, 96))
                    alone()
                    own.mark(pool.tensor_copy(CO[gc % 2][:, s, j, 0:2], U[:, SEQ:SEQ + 2]))
                    pool.tensor_copy(CO[gc % 2][:, s, j, 2:18].rearrange("p (b x) -> p b x", x=2),
                                     U[:, 2 + SEQ:UW].rearrange("p (b x) -> p b x", x=6)[:, :, 4:6]).then_inc(co_ready, 1)
            pool.wait_ge(co_ready, at(PAIR * (gc + 1), it, 16))
            own.wait()
            alone()
            dst = cout[:, :, bass.ds(g * GT, GT), :] if it is not None else cout[:, :, g * GT:(g + 1) * GT, :]
            pool.dma_start(dst, CO[gc % 2][:, :, :, :]).then_inc(co_stored, 16)
        own = Order(pool, pool_own)
        keep_rows(0, 0, 0)
        with pool.Fori(0, (NG - 1) // 2) as it:
            own.enter(it, 16)
            for p in range(2):
                keep_rows(it * 2 + (1 + p), 1 + p, 2 * PAIR + 48 * p, it)
            own.leave((NG - 1) // 2)
        for m in range(KT):
            add_squares(KT + m, first=m == 0)
        pool.wait_ge(co_stored, 16 * NG)
        pool.wait_ge(head_stored, 64 * HEADS)
        pool.wait_ge(state_stored, 16 * GH)
        pool.wait_ge(sstate_stored, 16 * GH)

    block.__exit__(None, None, None)


def _multiplicity(d):
    return sum(((d >= 0) & (d <= w) & (d % s == 0)).astype(np.int64) for w, s in ((128, 1), (512, 4), (2048, 16)))


def _bias(d, ok=True):
    c = np.where(ok, _multiplicity(d), 0)
    out = []
    for h in range(HEADS):
        slope = 2.0 ** (-8.0 * (h + 1) / HEADS)
        out.append(np.where(c > 0, -slope * d + np.log(np.maximum(c, 1)), NEG))
    out.append(out[-1])
    return np.stack(out).astype(np.float32)


def _constants():
    p = np.arange(P)
    tab_prompt = _bias(p[:, None] + (SEQ - P) - np.arange(SEQ)[None, :])
    pos = np.concatenate([
        (PAST - NEAR + 4 * np.arange(P)[None, :] + np.arange(4)[:, None]).ravel(),
        (16 * np.arange(FAR)[None, :] + np.arange(4)[:, None]).ravel(),
        PAST + np.arange(SAMP) % NQ])
    owner = np.concatenate([np.full(NKEY - SAMP, -1), np.arange(SAMP) // NQ])
    r = np.arange(SAMP)
    ok = (owner[None, :] < 0) | (owner[None, :] == r[:, None] // NQ)
    tab_sample = _bias(PAST + (r % NQ)[:, None] - pos[None, :], ok)
    t = np.arange(T)
    start = np.where(t < SEQ, t % CH == 0, (t - SEQ) % NQ == 0)
    return {
        "tab_prompt": tab_prompt,
        "tab_sample": tab_sample,
        "reset": np.repeat(np.where(start, 0.0, 1.0)[None, :], P, 0).astype(np.float32),
        "pair_mask": ((p[:, None] // CH == p[None, :] // CH) & (p[:, None] <= p[None, :])).astype(np.float32),
        "sample_mask": ((r[:, None] // NQ == r[None, :] // NQ) & (r[:, None] <= r[None, :])).astype(np.float32),
        "row_mask": (r[:, None] // NQ == np.arange(NB)[None, :]).astype(np.float32),
        "ident": np.eye(P, dtype=np.float32),
        "ones": np.ones((P, P), np.float32),
    }


_OUTS = {
    "y_t": (P, KT, T), "state_prompt": (GH, DK, DV), "state_sample": (NB, GH, DK, DV),
    "k_prompt_t": (HEADS, HD, SEQ), "k_sample": (NB, PAST, HEADS, HD), "v_prompt": (SEQ, HEADS, HD),
    "v_sample": (NB, PAST, HEADS, HD), "conv_out": (P, 2 * FT, 18),
}


def kernel(**inputs):
    import concourse.bacc as _bacc
    from concourse.bass_utils import run_bass_kernel_spmd as _run

    def tiles(v):
        v = np.asarray(v)
        return v.reshape(*v.shape[:-1], -1, P)

    x = np.concatenate([np.asarray(inputs["x_prompt"])[0], np.asarray(inputs["x_sample"]).reshape(SAMP, D)])
    conv = np.asarray(inputs["state_ffn_conv"])[0].reshape(NB * 2, 2 * FT, P)
    arrays = {
        "x_t": x.reshape(T, KT, P).transpose(2, 1, 0),
        "state_gla": np.asarray(inputs["state_gla"])[0],
        "cache_swa_k": np.asarray(inputs["cache_swa_k"])[0],
        "cache_swa_v": np.asarray(inputs["cache_swa_v"])[0],
        "conv_in": conv.transpose(2, 1, 0),
        "g_attn": tiles(inputs["g_attn_norm"])[0].T, "g_ffn": tiles(inputs["g_ffn_norm"])[0].T,
        "g_final": tiles(inputs["g_final"]).T, "g_gla": tiles(inputs["g_gla_norm"])[0].T,
        "b_gate": tiles(inputs["b_gate"])[0].T,
        "w_in": np.asarray(inputs["w_in"])[0], "w_gate": np.asarray(inputs["w_gate_up"])[0],
        "w_out": np.asarray(inputs["w_out"])[0], "w_up": np.asarray(inputs["w_up"])[0],
        "w_down": np.asarray(inputs["w_down"])[0],
        "w_conv": tiles(inputs["w_conv"])[0].transpose(2, 0, 1),
        "b_conv": tiles(inputs["b_conv"])[0].T,
        **_constants(),
    }
    arrays = {k: np.ascontiguousarray(v) for k, v in arrays.items()}
    nc = _bacc.Bacc("TRN2", target_bir_lowering=False, num_devices=1)
    A = {k: nc.dram_tensor(f"in_{k}", v.shape, mybir.dt.from_np(v.dtype), kind="ExternalInput").ap() for k, v in arrays.items()}
    O = {k: nc.dram_tensor(f"out_{k}", s, F32, kind="ExternalOutput").ap() for k, s in _OUTS.items()}
    build(nc, A, O)
    r = _run(nc, [{f"in_{k}": v for k, v in arrays.items()}], core_ids=[0]).results[0]
    got = {k: np.asarray(r[f"out_{k}"]) for k in _OUTS}
    y = got["y_t"].transpose(2, 1, 0).reshape(T, D)
    rows = got["conv_out"].transpose(2, 1, 0).reshape(18, 2 * DFF)
    return (y[:SEQ][None], y[SEQ:].reshape(NB, NQ, D),
            got["state_prompt"][None, None], got["state_sample"][None],
            got["k_prompt_t"].transpose(2, 0, 1)[None, None], got["k_sample"][None],
            got["v_prompt"][None, None], got["v_sample"][None],
            rows[:2][None, None], rows[2:].reshape(NB, 2, 2 * DFF)[None])
```
